# Optimizing a Trainium2 kernel written in Bass

```python
import jax
import jax.numpy as jnp
from jax import lax
import numpy as np

D_MODEL = 1024
BATCH = 1
SEQ = 2048
DEPTH = 2
DEC_BATCH = 8
DEC_SEQ = 4
PAST_LEN = 2048
PAGE_SIZE = 128

A_HEADS = 8
A_KV_HEADS = 2
A_GROUP = A_HEADS // A_KV_HEADS
A_HEAD_DIM = 64
WINDOW = 128
A_ROT_DIM = A_HEAD_DIM // 4
ROPE_THETA_A = 500000.0
B_HEADS = 4
B_DK = 128
B_DV = 128
RET_CHUNK = 128
ROPE_THETA_B = 10000.0
EPS = 1e-6

A_WIDTH = A_HEADS * A_HEAD_DIM
A_KV_WIDTH = A_KV_HEADS * A_HEAD_DIM
B_QK_WIDTH = B_HEADS * B_DK
B_V_WIDTH = B_HEADS * B_DV
MIX_WIDTH = A_WIDTH + B_V_WIDTH
SPLITS = (A_WIDTH, A_KV_WIDTH, A_KV_WIDTH, A_WIDTH, B_QK_WIDTH, B_QK_WIDTH, B_V_WIDTH, B_V_WIDTH)
IN_WIDTH = A_WIDTH + 2 * A_KV_WIDTH + A_WIDTH + 2 * B_QK_WIDTH + 2 * B_V_WIDTH

kernel_name = 'hymba_swa_sink_retention_step'

def rms_norm(x, g=None):
    xf = x.astype(jnp.float32)
    y = xf * lax.rsqrt(jnp.mean(xf * xf, axis=-1, keepdims=True) + EPS)
    if g is not None:
        y = y * g.astype(jnp.float32)
    return y.astype(x.dtype)

def rotary(x, pos, rot_dim, theta):
    half = rot_dim // 2
    inv_freq = theta ** (-jnp.arange(half, dtype=jnp.float32) / half)
    ang = pos.astype(jnp.float32)[:, None] * inv_freq[None, :]
    cos = jnp.cos(ang)[:, None, :]
    sin = jnp.sin(ang)[:, None, :]
    xr = x[..., :rot_dim].astype(jnp.float32)
    x1, x2 = xr[..., :half], xr[..., half:]
    rot = jnp.concatenate([x1 * cos - x2 * sin, x2 * cos + x1 * sin], axis=-1)
    return jnp.concatenate([rot.astype(x.dtype), x[..., rot_dim:]], axis=-1)

def project(x, pos, w_in, norm_g, q_norm_g, k_norm_g):
    N, T, _ = x.shape
    h = rms_norm(x, norm_g)
    p = jnp.einsum('ntd,de->nte', h, w_in)
    offs = np.cumsum(SPLITS)[:-1].tolist()
    qa, ka, va, ga, qb, kb, vb, gb = jnp.split(p, offs, axis=-1)
    qa = rotary(rms_norm(qa.reshape(N, T, A_HEADS, A_HEAD_DIM), q_norm_g), pos, A_ROT_DIM, ROPE_THETA_A)
    ka = rotary(rms_norm(ka.reshape(N, T, A_KV_HEADS, A_HEAD_DIM), k_norm_g), pos, A_ROT_DIM, ROPE_THETA_A)
    va = va.reshape(N, T, A_KV_HEADS, A_HEAD_DIM)
    qb = rotary(qb.reshape(N, T, B_HEADS, B_DK), pos, B_DK, ROPE_THETA_B)
    kb = rotary(kb.reshape(N, T, B_HEADS, B_DK), pos, B_DK, ROPE_THETA_B) * (B_DK ** -0.5)
    vb = vb.reshape(N, T, B_HEADS, B_DV)
    return qa, ka, va, ga, qb, kb, vb, gb

def attend_with_sinks(q, kk, vv, mask, sinks):
    s = jnp.einsum('...qgrd,...kgd->...grqk', q, kk, preferred_element_type=jnp.float32) * (A_HEAD_DIM ** -0.5)
    s = jnp.where(mask, s, -jnp.inf)
    sk = sinks.astype(jnp.float32).reshape(A_KV_HEADS, A_GROUP)[:, :, None, None]
    m = jnp.maximum(jnp.max(s, axis=-1, keepdims=True), sk)
    p = jnp.exp(s - m)
    denom = jnp.sum(p, axis=-1, keepdims=True) + jnp.exp(sk - m)
    p = (p / denom).astype(vv.dtype)
    return jnp.einsum('...grqk,...kgd->...qgrd', p, vv)

def swa_prompt(qa, ka, va, sinks):
    N, T = qa.shape[:2]
    nb = T // WINDOW
    qblk = qa.reshape(N, nb, WINDOW, A_KV_HEADS, A_GROUP, A_HEAD_DIM)
    kblk = ka.reshape(N, nb, WINDOW, A_KV_HEADS, A_HEAD_DIM)
    vblk = va.reshape(N, nb, WINDOW, A_KV_HEADS, A_HEAD_DIM)
    kk = jnp.concatenate([jnp.concatenate([jnp.zeros_like(kblk[:, :1]), kblk[:, :-1]], axis=1), kblk], axis=2)
    vv = jnp.concatenate([jnp.concatenate([jnp.zeros_like(vblk[:, :1]), vblk[:, :-1]], axis=1), vblk], axis=2)
    qi = jnp.arange(WINDOW)[:, None] + WINDOW
    kj = jnp.arange(2 * WINDOW)[None, :]
    diff = qi - kj
    band = (diff >= 0) & (diff < WINDOW)
    has_prev = (jnp.arange(nb) > 0)[:, None, None] | (kj >= WINDOW)[None]
    mask = (band[None] & has_prev)[:, None, None]
    o = attend_with_sinks(qblk, kk, vv, mask, sinks)
    return o.reshape(N, T, A_WIDTH)

def swa_sample(qa, ka, va, cache_k, cache_v, sinks):
    N, T = qa.shape[:2]
    w_buf = cache_k.shape[1]
    kk = jnp.concatenate([cache_k.astype(ka.dtype), ka], axis=1)
    vv = jnp.concatenate([cache_v.astype(va.dtype), va], axis=1)
    diff = jnp.arange(T)[:, None] + w_buf - jnp.arange(w_buf + T)[None, :]
    mask = (diff >= 0) & (diff < WINDOW)
    o = attend_with_sinks(qa.reshape(N, T, A_KV_HEADS, A_GROUP, A_HEAD_DIM), kk, vv, mask, sinks)
    return o.reshape(N, T, A_WIDTH), kk[:, -w_buf:], vv[:, -w_buf:]

def retention_log_decay():
    return jnp.log(1.0 - 2.0 ** (-5.0 - jnp.arange(B_HEADS, dtype=jnp.float32)))

def retention_chunk(S, q, k, v):
    C = q.shape[1]
    lg = retention_log_decay()
    idx = jnp.arange(C, dtype=jnp.float32)
    diff = idx[:, None] - idx[None, :]
    decay = jnp.where(diff >= 0, jnp.exp(lg[:, None, None] * jnp.maximum(diff, 0.0)), 0.0)
    qf = q.astype(jnp.float32)
    kf = k.astype(jnp.float32)
    vf = v.astype(jnp.float32)
    scores = jnp.einsum('nihd,njhd->nhij', qf, kf) * decay
    inner = jnp.einsum('nhij,njhv->nihv', scores, vf)
    q_dec = jnp.exp(lg[None, :] * (idx[:, None] + 1.0))
    cross = jnp.einsum('nihd,nhdv->nihv', qf, S) * q_dec[None, :, :, None]
    k_dec = jnp.exp(lg[None, :] * (C - 1.0 - idx[:, None]))
    S_new = jnp.exp(lg * C)[None, :, None, None] * S + jnp.einsum('njhd,njhv->nhdv', kf * k_dec[None, :, :, None], vf)
    return S_new, inner + cross

def retention_prompt(qb, kb, vb):
    N, T = qb.shape[:2]
    C = min(RET_CHUNK, T)
    nc = T // C

    def to_chunks(a):
        return a.reshape(N, nc, C, *a.shape[2:]).swapaxes(0, 1)

    S0 = jnp.zeros((N, B_HEADS, B_DK, B_DV), jnp.float32)
    S, o = lax.scan(lambda S, xs: retention_chunk(S, *xs), S0, (to_chunks(qb), to_chunks(kb), to_chunks(vb)))
    return o.swapaxes(0, 1).reshape(N, T, B_HEADS, B_DV), S

def merge(x, attn, ret, ga, gb, w_out):
    N, T = x.shape[:2]
    ret = rms_norm(ret).reshape(N, T, B_V_WIDTH).astype(x.dtype)
    mixed = jnp.concatenate([jax.nn.silu(ga) * attn, jax.nn.silu(gb) * ret], axis=-1)
    return x + jnp.einsum('nte,ed->ntd', mixed, w_out)

def setup_inputs(seed: int = 0) -> dict:
    key = jax.random.key(seed)
    ks = jax.random.split(key, 11)
    w_buf = min(WINDOW, PAST_LEN)
    f32 = jnp.float32
    return {
        'x_prompt': jax.random.normal(ks[0], (BATCH, SEQ, D_MODEL), f32),
        'x_sample': jax.random.normal(ks[1], (DEC_BATCH, DEC_SEQ, D_MODEL), f32),
        'cache_swa_k': jax.random.normal(ks[2], (DEPTH, DEC_BATCH, w_buf, A_KV_HEADS, A_HEAD_DIM), f32),
        'cache_swa_v': jax.random.normal(ks[3], (DEPTH, DEC_BATCH, w_buf, A_KV_HEADS, A_HEAD_DIM), f32),
        'state_ret': 0.5 * jax.random.normal(ks[4], (DEPTH, DEC_BATCH, B_HEADS, B_DK, B_DV), f32),
        'w_in': jax.random.normal(ks[5], (DEPTH, D_MODEL, IN_WIDTH), f32) * (D_MODEL ** -0.5),
        'w_out': jax.random.normal(ks[6], (DEPTH, MIX_WIDTH, D_MODEL), f32) * (MIX_WIDTH ** -0.5),
        'norm_g': 1.0 + 0.02 * jax.random.normal(ks[7], (DEPTH, D_MODEL), f32),
        'q_norm_g': 1.0 + 0.02 * jax.random.normal(ks[8], (DEPTH, A_HEAD_DIM), f32),
        'k_norm_g': 1.0 + 0.02 * jax.random.normal(ks[9], (DEPTH, A_HEAD_DIM), f32),
        'sinks': 0.5 * jax.random.normal(ks[10], (DEPTH, A_HEADS), f32),
    }

def reference(x_prompt, x_sample, cache_swa_k, cache_swa_v, state_ret, w_in, w_out, norm_g, q_norm_g, k_norm_g, sinks):
    pos_p = jnp.arange(x_prompt.shape[1], dtype=jnp.int32)
    pos_s = PAST_LEN + jnp.arange(x_sample.shape[1], dtype=jnp.int32)
    w_p = min(WINDOW, x_prompt.shape[1])
    xp, xs = x_prompt, x_sample
    kp_l, vp_l, sp_l, ks_l, vs_l, ss_l = [], [], [], [], [], []
    for l in range(DEPTH):
        qa, ka, va, ga, qb, kb, vb, gb = project(xp, pos_p, w_in[l], norm_g[l], q_norm_g[l], k_norm_g[l])
        attn = swa_prompt(qa, ka, va, sinks[l])
        ret, S = retention_prompt(qb, kb, vb)
        xp = merge(xp, attn, ret, ga, gb, w_out[l])
        kp_l.append(ka[:, -w_p:])
        vp_l.append(va[:, -w_p:])
        sp_l.append(S.astype(xp.dtype))
        qa, ka, va, ga, qb, kb, vb, gb = project(xs, pos_s, w_in[l], norm_g[l], q_norm_g[l], k_norm_g[l])
        attn, k_buf, v_buf = swa_sample(qa, ka, va, cache_swa_k[l], cache_swa_v[l], sinks[l])
        S, ret = retention_chunk(state_ret[l].astype(jnp.float32), qb, kb, vb)
        xs = merge(xs, attn, ret, ga, gb, w_out[l])
        ks_l.append(k_buf)
        vs_l.append(v_buf)
        ss_l.append(S.astype(xs.dtype))
    return (xp, xs, jnp.stack(kp_l), jnp.stack(vp_l), jnp.stack(sp_l), jnp.stack(ks_l), jnp.stack(vs_l), jnp.stack(ss_l))


_drawn_inputs = setup_inputs


def setup_inputs(seed=0):
    import zlib

    import numpy as np

    out = dict(_drawn_inputs(seed))
    spreads = {}
    factors = {'q_norm_g': 8.0, 'sinks': 47.389}
    for name, (base, spread) in spreads.items():
        noise = np.random.default_rng([zlib.crc32(name.encode()), seed]).standard_normal(out[name].shape)
        drawn = base * np.exp(spread * noise) if base else spread * noise
        out[name] = jnp.asarray(drawn.astype(out[name].dtype))
    for name, factor in factors.items():
        out[name] = (out[name] * factor).astype(out[name].dtype)
    return out
```

```python
import concourse.bass as bass
from concourse import mybir
from contextlib import ExitStack

F32 = mybir.dt.float32
F16 = mybir.dt.float16
BF16 = mybir.dt.bfloat16
I32 = mybir.dt.int32
U16 = mybir.dt.uint16
ALU = mybir.AluOpType
ACT = mybir.ActivationFunctionType
AX = mybir.AxisListType

D_MODEL, SEQ, DEPTH, DEC_BATCH, DEC_SEQ, PAST = 1024, 2048, 2, 8, 4, 2048
A_HEADS, A_KV, A_DIM, WINDOW = 8, 2, 64, 128
A_GROUP = A_HEADS // A_KV
ROT = A_DIM // 4
B_HEADS, DK, DV = 4, 128, 128
EPS = 1e-6
P = 128
KT = D_MODEL // P
TILES = SEQ // P
STEPS = TILES + 1
NS = DEC_BATCH * DEC_SEQ
ROWS = SEQ + NS
A_W, KV_W, B_W = A_HEADS * A_DIM, A_KV * A_DIM, B_HEADS * DK
IN_W = 2 * A_W + 2 * KV_W + 4 * B_W
MIX_W = A_W + B_W
N_A = 2 * A_W + 2 * KV_W
N_B = 4 * 2 * DK
N_O = D_MODEL
H_SCALE = 2.0 ** 10
TOP = 2.0 ** -14
TINY = 1e-30
NEG = -1e30
MAGIC = 1597463007.0
NEWTON = 3
RSQRT_LINKS = 2 + 3 * NEWTON
CH_A = ((0, A_W), (A_W, 2 * KV_W), (A_W + 2 * KV_W, A_W))
CH_2 = ((0, 512), (512, 512))
PIECE0 = {"A": 0, "B0": 3 * STEPS, "B1": 5 * STEPS, "O": 7 * STEPS}
PIECES = 9 * STEPS
APIECE0 = {"A": 0, "B0": 3 * STEPS, "B1": 4 * STEPS}
APIECES = 5 * STEPS
MIX_OUT = (26, 25)
MIX_OUT0 = {"A": (0, 0), "B0": (9, 8), "B1": (17, 17)}
KEYS = DEC_BATCH * WINDOW


def lam(h):
    return 1.0 - 2.0 ** (-5.0 - h)


def bfloat16_bits(x):
    import numpy as np
    return (np.ascontiguousarray(x, dtype=np.float32).view(np.uint32) >> 16).astype(np.uint16)


def constants():
    import numpy as np
    f = np.float32
    c = {}
    pos = np.arange(SEQ)
    ps = PAST + np.arange(NS) % DEC_SEQ
    for name, theta, half in (("a", 500000.0, ROT // 2), ("b", 10000.0, DK // 2)):
        inv = (f(theta) ** (-np.arange(half, dtype=f) / f(half))).astype(f)
        for tag, p in (("p", pos), ("s", ps)):
            ang = (p.astype(f)[:, None] * inv[None, :]).astype(f).astype(np.float64)
            t = np.stack([np.cos(ang), np.sin(ang)], 1).astype(f)
            if tag == "p":
                t = t.reshape(TILES, P, 2, half).transpose(1, 0, 2, 3)
            c[f"rope_{name}{tag}"] = np.ascontiguousarray(t)
    i = np.arange(P)[:, None]
    j = np.arange(P)[None, :]
    cur = np.where(j <= i, 0.0, NEG)
    prev = np.where(j > i, 0.0, NEG)
    none = np.full((P, P), NEG)
    m = np.stack([np.concatenate(x, 1) for x in ((cur, prev), (prev, cur), (none, cur))], 1)
    c["mask_a"] = bfloat16_bits(m)
    tok = np.arange(P) % NS
    b, ti = tok // DEC_SEQ, tok % DEC_SEQ
    kb = np.concatenate([np.arange(KEYS) // WINDOW, np.arange(NS) // DEC_SEQ])
    kj = np.concatenate([np.arange(KEYS) % WINDOW, WINDOW + np.arange(NS) % DEC_SEQ])
    diff = ti[:, None] + WINDOW - kj[None, :]
    ok = (b[:, None] == kb[None, :]) & (diff >= 0) & (diff < WINDOW)
    c["mask_s"] = bfloat16_bits(np.where(ok, 0.0, NEG))
    dec = np.zeros((P, B_HEADS, P))
    decs = np.zeros((NS, B_HEADS, NS))
    cols = np.zeros((P, 32))
    r = np.arange(P)
    rs = np.arange(NS) % DEC_SEQ
    bs = np.arange(NS) // DEC_SEQ
    for h in range(B_HEADS):
        dec[:, h, :] = np.where(j >= i, lam(h) ** -(i + 1.0), 0.0) * DK ** -0.5
        ok = (bs[:, None] == bs[None, :]) & (rs[None, :] >= rs[:, None])
        decs[:, h, :] = np.where(ok, lam(h) ** -(rs[:, None] + 1.0), 0.0) * DK ** -0.5
        q, k = lam(h) ** (r + 1.0), lam(h) ** (P - 1.0 - r) * DK ** -0.5
        qs, ks = lam(h) ** (rs + 1.0), lam(h) ** (DEC_SEQ - 1.0 - rs) * DK ** -0.5
        cols[:, h], cols[:, 4 + h], cols[:, 8 + h] = q * q / DV, q, k
        cols[:NS, 12 + h], cols[:NS, 16 + h], cols[:NS, 20 + h] = qs * qs / DV, qs, ks
    cols[:NS, 24:32] = bs[:, None] == np.arange(DEC_BATCH)[None, :]
    c["decay"], c["decay_s"], c["cols"] = dec.astype(f), decs.astype(f), cols.astype(f)
    c["ident"] = np.eye(P, dtype=f)
    return c


class Step:

    def __init__(self, c, i=0):
        self.v, self.half, self.par = c + 2 * i, c // 2 + i, c % 2
        self.fixed = isinstance(i, int)
        self.sample = self.fixed and c == 0
        self.first = self.fixed and c == 1
        self.rows = NS if self.sample else P
        self.tile = self.v - 1
        self.col = SEQ if self.sample else self.tile * P
        self.c, self.i = c, i

    def __add__(self, d):
        return Step(self.c + d, self.i)

    def __sub__(self, d):
        return Step(self.c - d, self.i)


class Chain:

    def __init__(self, eng, sem, links, times):
        self.eng, self.sem, self.links, self.base, self.n = eng, sem, links, times * links, 0

    def __call__(self, ins):
        self.n += 1
        ins.then_inc(self.sem, 1)
        self.eng.wait_ge(self.sem, self.base + self.n)

    def end(self, unwaited=0):
        assert self.n + unwaited == self.links, (self.n, self.links)


def trunk(nc, x_prompt, x_sample, cache_k, cache_v, state_ret, w_in, w_out, norm_g, q_g, k_g, sinks,
          rope_ap, rope_as, rope_bp, rope_bs, mask_a, mask_s, decay, decay_s, cols, ident,
          y_p, y_s, nk_p, nv_p, nst_p, nk_s, nv_s, nst_s, mixed):
    with ExitStack() as ctx:
        def sb(name, shape, dt=F32):
            return ctx.enter_context(nc.sbuf_tensor(name, shape, dt))

        def sem(name):
            return ctx.enter_context(nc.semaphore(name))

        hT = sb("hT", [P, 2, KT, ROWS], F16)
        w_a = sb("w_a", [P, KT * N_A])
        w_b = sb("w_b", [P, KT * N_B])
        w_tmp = sb("w_tmp", [P, 512])
        land = sb("land", [P, 2, 2 * A_W + 2 * KV_W])
        mix = sb("mix", [P, 2, A_W])
        r1 = sb("r1", [P, 4096])
        r2 = sb("r2", [P, 4384])
        t_rap, t_ras = sb("t_rap", [P, TILES, 2, ROT // 2]), sb("t_ras", [NS, 2, ROT // 2])
        t_rbp, t_rbs = sb("t_rbp", [P, TILES, 2, DK // 2]), sb("t_rbs", [NS, 2, DK // 2])
        t_ma, t_ms = sb("t_ma", [P, 3, 2 * P], U16), sb("t_ms", [P, KEYS + NS], U16)
        t_dec, t_decs = sb("t_dec", [P, B_HEADS, P]), sb("t_decs", [NS, B_HEADS, NS])
        t_cols, eye = sb("t_cols", [P, 32]), sb("eye", [P, P])
        g_all = sb("g_all", [P, DEPTH, KT])
        qk_all = sb("qk_all", [P, DEPTH, 2, A_DIM])
        sk_all = sb("sk_all", [P, DEPTH, A_HEADS])
        sks_all = sb("sks_all", [P, DEPTH, A_KV])
        qk_g, sk, sks = sb("qk_g", [P, 2, A_DIM]), sb("sk", [P, A_HEADS]), sb("sks", [P, A_KV])
        nsk, nsks = sb("nsk", [P, A_HEADS]), sb("nsks", [P, A_KV])
        ones = sb("ones", [P, KT])
        g_cur = sb("g_cur", [P, KT])
        w_mx, w_m1, w_am, w_q, w_s, w_gs = (sb(n, [P, m]) for n, m in (
            ("w_mx", KT), ("w_m1", 1), ("w_am", 1), ("w_q", 1), ("w_s", 1), ("w_gs", KT)))
        cs = {k: sb(f"cs_{k}", [P, 8]) for k in ("A", "B0", "B1", "O")}
        ss, rs, rt = sb("ss", [P, 10]), sb("rs", [P, 2, 10]), sb("rt", [P, 10])
        rp1, rp2 = sb("rp1", [P, 10, 2, ROT // 2]), sb("rp2", [P, 10, 2, ROT // 2])
        mr, nm, sd, es, rsum, rr = (sb(n, [P, 2, A_GROUP]) for n in ("mr", "nm", "sd", "es", "rsum", "rr"))
        oss, oms, oy, ot = (sb(n, [P, 2]) for n in ("oss", "oms", "oy", "ot"))
        mq, mqq, minv, mdd = sb("mq", [P, 1]), sb("mqq", [P, 2]), sb("minv", [P, 2]), sb("mdd", [P, 2])
        xss, xms, xy, xt = sb("xss", [P, 1]), sb("xms", [P, 1]), sb("xy", [P, 2]), sb("xt", [P, 1])

        ck = r1[:, 0:1024].rearrange("p (b c) -> p b c", c=KV_W)
        cv = r1[:, 1024:2048].rearrange("p (b c) -> p b c", c=KV_W)
        kts = r1[:, 2048:3072]
        knew = r1[:, 3072:3072 + 2 * NS].rearrange("p (g n) -> p g n", g=2)
        stS = r1[:, 0:2048].rearrange("p (h b v) -> p h b v", h=2, b=DEC_BATCH)
        qtm = r1[:, 2048:2048 + 2 * 288].rearrange("p (h n) -> p h n", h=2)
        t1 = r1[:, 3072:3584]
        t2 = r1[:, 3584:4096]
        mxt = r1[:, 0:2048].rearrange("p (b n) -> p b n", b=2)
        xt_ = r1[:, 2048:4096].rearrange("p (b n) -> p b n", b=2)
        sq = r2[:, 0:640]
        kT = r2[:, 640:896]
        qT = r2[:, 896:1408]
        vr = r2[:, 1408:1664].rearrange("p (b n) -> p b n", b=2)
        vd = r2[:, 1664:2176].rearrange("p (b n) -> p b n", b=2)
        prob = r2[:, 2176:3232]
        pT = r2[:, 3232:4384]
        qkT = r2[:, 0:512]
        osq = r2[:, 640:896]
        state = (r2[:, 896:1152], r2[:, 1408:1664])
        stm = r2[:, 1152:1408]
        vbd = r2[:, 2176:2176 + 2048].rearrange("p (h b v) -> p h b v", h=2, b=DEC_BATCH)
        xn = r2[:, 288:1312]
        mT = tuple(r2[:, o:o + 1024].bitcast(F16).rearrange("p (k e t) -> p k e t", k=KT, e=2)
                   for o in (2336, 1312))
        msc = r2[:, 3360:4384]

        PA, PB, TK, S0, S1, X0, X1, OB = (
            ctx.enter_context(nc.psum_tensor(n, [P, 512], F32))
            for n in ("PA", "PB", "TK", "S0", "S1", "X0", "X1", "OB"))
        PP, SS, XX = (PA, PB), (S0, S1), (X0, X1)

        c_ld, xy_cp = sem("consts_loaded"), sem("x_copied")
        init = sem("memsets_done")
        pe_piece, act_piece, dve_piece = sem("pe_piece"), sem("act_piece"), sem("dve_piece")
        w_ld = (sem("w_loaded_lo"), sem("w_loaded_hi"))
        w_max, w_all, w_sc, w_rd = sem("w_max"), sem("w_allreduced"), sem("w_scales"), sem("w_ready")
        a_qk, a_tk, a_te = sem("a_qk_ready"), sem("a_transposed"), sem("a_transposes_out")
        s_ct, s_ce = sem("cached_keys_transposed"), sem("cached_keys_out")
        a_s, a_sm, a_ex = sem("a_scores"), sem("a_masked"), sem("a_probs")
        a_pt, a_po, a_pv, a_mx = sem("a_probsT"), sem("a_probsT_out"), sem("a_pv"), sem("a_mixed")
        b_qk, b_tk, b_te = sem("b_qk_ready"), sem("b_transposed"), sem("b_transposes_out")
        b_st, b_dm, b_o = sem("b_scoresT"), sem("b_decayed"), sem("b_out")
        b_su, b_sq, b_mx, b_vb = sem("b_state"), sem("b_squares"), sem("b_mixed"), sem("b_vbd")
        mix_out = (sem("mix_out0"), sem("mix_out1"))
        kv_out, st_out, sts_out = sem("kv_out"), sem("state_out"), sem("sample_state_out")
        kvs_out, kc_out = sem("kv_sample_out"), sem("cache_shift_out")
        ckv_ld, sts_ld = sem("cache_loaded"), sem("sample_state_loaded")
        mx_ld, x_ld = (sem("mixed_loaded0"), sem("mixed_loaded1")), (sem("x_loaded0"), sem("x_loaded1"))
        y_out = (sem("y_out0"), sem("y_out1"))
        o_sc, o_ms, o_tm, o_hi, o_lo = (sem(n) for n in (
            "o_scale", "o_scaled", "o_transposed", "o_hi", "o_lo"))
        h_sq, h_rs, h_xn, h_t, h_hi, h_lo = (sem(n) for n in (
            "h_squares", "h_rstd", "h_normed", "h_transposed", "h_hi", "h_lo"))
        alone_count = sem("alone_count")
        ch_wm, ch_ws, ch_wp, ch_an, ch_asm, ch_amx, ch_ams, ch_bo, ch_om, ch_ou, ch_h, ch_l = (sem(n) for n in (
            "chain_w_max", "chain_w_scale", "chain_w_pool", "chain_a_norm", "chain_a_softmax",
            "chain_a_mix", "chain_a_mix_sample", "chain_b_out", "chain_o_scale", "chain_o_unscale", "chain_h", "chain_layer"))

        BLOCKS = ("A", "B0", "B1", "O")
        SLOT = {"A": w_a, "B0": w_b, "B1": w_a, "O": w_b}
        WIDTH = {"A": N_A, "B0": N_B, "B1": N_B, "O": N_O}
        CH = {"A": CH_A, "B0": CH_2, "B1": CH_2, "O": CH_2}

        def hb(ph):
            return int(ph[1])

        def an(L, s):
            return L * STEPS + s.v

        def bn(ph, L, s):
            return (L * 2 + hb(ph)) * STEPS + s.v

        def hn(L, s):
            return (L + 1) * STEPS + s.v

        def wn(L, kind):
            return L * 4 + BLOCKS.index(kind)

        def lpar(ph, s):
            return (s.par + 1) % 2 if ph == "B0" else s.par

        def mix_count(ph, L, s):
            p = lpar(ph, s)
            return L * MIX_OUT[p] + MIX_OUT0[ph][p] + s.half + 1

        def piece(ph, L, s, p):
            return L * PIECES + PIECE0[ph] + s.v * (3 if ph == "A" else 2) + p

        def bank(ph, s, p):
            if ph == "A":
                return PP[(s.par * 3 + p) % 2]
            return PP[(p + 1) % 2]

        def apiece(ph, L, s, p):
            return L * APIECES + APIECE0[ph] + (s.v * 3 + p if ph == "A" else s.v)

        def w16(kind, k, c, part):
            c0, n = CH[kind][c]
            o = (k * WIDTH[kind] + c0) * 2 + part * n
            return SLOT[kind][:, :].bitcast(F16)[:, o:o + n]

        def raw(kind, k, c=None):
            c0, n = (0, WIDTH[kind]) if c is None else CH[kind][c]
            o = k * WIDTH[kind] + c0
            return SLOT[kind][:, o:o + n]

        def hcols(s):
            return slice(s.col, s.col + s.rows) if s.fixed else bass.ds(s.col, P)

        def alone(eng, semaphore, value):
            eng.wait_ge(semaphore, value)
            eng.sem_inc(alone_count, 1)

        block = ctx.enter_context(nc.Block())

        @block.tensor
        def _(pe):
            def proj(ph, L, s, p, half):
                out = bank(ph, s, p)
                n = CH[ph][p][1]
                j = piece(ph, L, s, p)
                if half == 0:
                    pe.wait_ge(dve_piece, j + 1 if ph == "A" and s.sample and p == 0 else j)
                    if ph == "O" and p == 0:
                        pe.wait_ge(o_lo, L * STEPS + s.v + 1)
                for k in range(half * KT // 2, (half + 1) * KT // 2):
                    for part, wpart in ((0, 0), (0, 1), (1, 0)):
                        if ph == "O":
                            lhs = mT[s.par][:, k, part, 0:s.rows]
                        else:
                            lhs = hT[:, part, k, hcols(s)]
                        last = nc.tensor.matmul(
                            out[0:s.rows, 0:n], lhs, w16(ph, k, p, wpart),
                            start=(k == 0 and part == 0 and wpart == 0),
                            stop=(k == KT - 1 and part == 1))
                if half == 1:
                    last.then_inc(pe_piece, 1)

            def a_T(L, s):
                pe.wait_ge(a_qk, an(L, s) + 1)
                if s.sample:
                    alone(pe, ckv_ld, (L + 1) * 32)
                    for g in range(A_KV):
                        for h in range(A_GROUP):
                            q, o = g * A_GROUP + h, (h * A_KV + g) * A_DIM
                            nc.tensor.transpose(TK[0:A_DIM, q * NS:(q + 1) * NS],
                                                land[0:NS, 0, o:o + A_DIM], eye[0:NS, 0:NS])
                        o = A_W + g * A_DIM
                        nc.tensor.transpose(TK[0:A_DIM, (A_HEADS + g) * NS:(A_HEADS + g + 1) * NS],
                                            land[0:NS, 0, o:o + A_DIM], eye[0:NS, 0:NS])
                    last = cached_keys(0)
                else:
                    if s.first:
                        pe.wait_ge(a_po, 2 * an(L, s))
                    for i in range(4):
                        nc.tensor.transpose(TK[:, i * P:(i + 1) * P], land[:, s.par, i * P:(i + 1) * P], eye[:, :])
                    if not s.first:
                        pe.wait_ge(a_sm, 2 * an(L, s))
                    last = nc.tensor.transpose(S0[:, 0:P], land[:, s.par, A_W:A_W + P], eye[:, :])
                last.then_inc(a_tk, 1)

            def cached_keys(g):
                for q in range(DEC_BATCH):
                    last = nc.tensor.transpose(XX[q // 4][0:A_DIM, (q % 4) * P:(q % 4 + 1) * P],
                                               ck[:, q, g * A_DIM:(g + 1) * A_DIM], eye[:, :])
                return last

            def a_S(L, s, g):
                n = an(L, s)
                pe.wait_ge(a_te, n + 1)
                if not (s.sample and g == 0):
                    pe.wait_ge(a_sm, 2 * n + g)
                if s.sample:
                    if g == 1:
                        pe.wait_ge(a_po, 2 * n + 1)
                    lhs = qT[0:A_DIM, g * P:(g + 1) * P]
                    for q in range(2):
                        nc.tensor.matmul(SS[q][:, :], lhs, kts[0:A_DIM, q * 512:(q + 1) * 512],
                                         start=True, stop=True)
                    last = nc.tensor.matmul(TK[:, 0:NS], lhs, knew[0:A_DIM, g, :], start=True, stop=True)
                else:
                    for h in range(A_GROUP):
                        r = slice(A_DIM * g, A_DIM * (g + 1))
                        last = nc.tensor.matmul(SS[h // 2][:, (h % 2) * 256:(h % 2) * 256 + 256],
                                                qT[r, h * P:(h + 1) * P], kT[r, :],
                                                start=True, stop=True)
                last.then_inc(a_s, 1)

            def a_PT(L, s, g):
                if s.sample and g == 0:
                    pe.wait_ge(s_ce, L + 1)
                pe.wait_ge(a_ex, 2 * an(L, s) + g + 1)
                for q in range(8):
                    last = nc.tensor.transpose(XX[q // 4][:, (q % 4) * P:(q % 4 + 1) * P],
                                               prob[:, q * P:(q + 1) * P], eye[:, :])
                if s.sample:
                    last = nc.tensor.transpose(TK[0:NS, P:2 * P], prob[:, KEYS:KEYS + NS], eye[:, :])
                last.then_inc(a_pt, 1)

            def a_PV(L, s, g):
                n = an(L, s)
                pe.wait_ge(a_po, 2 * n + g + 1)
                if not (s.sample and g == 0):
                    pe.wait_ge(a_mx, 2 * n + g)
                if s.sample:
                    for q in range(DEC_BATCH):
                        nc.tensor.matmul(OB[:, 0:A_DIM], pT[:, q * P:(q + 1) * P],
                                         cv[:, q, g * A_DIM:(g + 1) * A_DIM], start=(q == 0), stop=False)
                    o = A_W + KV_W + g * A_DIM
                    last = nc.tensor.matmul(OB[:, 0:A_DIM], pT[0:NS, KEYS:KEYS + P],
                                            land[0:NS, 0, o:o + A_DIM], start=False, stop=True)
                else:
                    for h in range(A_GROUP):
                        for q in range(2):
                            o = (h * 2 + q) * P
                            last = nc.tensor.matmul(OB[:, h * A_DIM:(h + 1) * A_DIM], pT[:, o:o + P],
                                                    vr[:, q, g * A_DIM:(g + 1) * A_DIM],
                                                    start=(q == 0), stop=(q == 1))
                last.then_inc(a_pv, 1)

            def b_T(ph, L, s):
                b, r = lpar(ph, s), s.rows
                alone(pe, b_qk, bn(ph, L, s) + 1)
                for i in range(4):
                    last = nc.tensor.transpose(TK[:, i * r:(i + 1) * r], land[0:r, b, i * P:(i + 1) * P],
                                               eye[0:r, 0:r])
                last.then_inc(b_tk, 1)

            def b_ST(ph, L, s):
                r = s.rows
                if s.first:
                    pe.wait_ge(b_su, bn(ph, L, s))
                pe.wait_ge(b_te, bn(ph, L, s) + 1)
                for h in range(2):
                    last = nc.tensor.matmul(S0[0:r, h * r:(h + 1) * r], qkT[:, (2 + h) * r:(3 + h) * r],
                                            qkT[:, h * r:(h + 1) * r], start=True, stop=True)
                last.then_inc(b_st, 1)

            def b_OS(ph, L, s):
                n, b, r, st = bn(ph, L, s), lpar(ph, s), s.rows, state[hb(ph)]
                pe.wait_ge(b_dm, n + 1)
                pe.wait_ge(act_piece, apiece(ph, L, s, 1) + 1)
                if not s.sample:
                    pe.wait_ge(b_su, n)
                    pe.wait_ge(b_mx, n)
                else:
                    pe.wait_ge(sts_ld, (L * 2 + hb(ph) + 1) * 32)
                    if hb(ph) == 1:
                        pe.wait_ge(b_mx, n)
                    alone(pe, b_vb, L * 2 + hb(ph) + 1)
                for h in range(2):
                    v = land[0:r, b, 512 + h * P:512 + (h + 1) * P]
                    nc.tensor.matmul(OB[0:r, h * P:(h + 1) * P], stm[0:r, h * r:(h + 1) * r], v,
                                     start=True, stop=False)
                    if s.sample:
                        for q in range(DEC_BATCH):
                            last = nc.tensor.matmul(OB[0:r, h * P:(h + 1) * P], qtm[:, h, q * NS:(q + 1) * NS],
                                                    stS[:, h, q, :], start=False, stop=(q == DEC_BATCH - 1))
                    else:
                        last = nc.tensor.matmul(OB[0:r, h * P:(h + 1) * P], qkT[:, h * P:(h + 1) * P],
                                                st[:, h * P:(h + 1) * P], start=False, stop=True)
                for h in range(2):
                    k = land[0:r, b, (2 + h) * P:(3 + h) * P]
                    if s.sample:
                        for q, bk in enumerate(((S1, X0), (X1, S0))[h]):
                            last = nc.tensor.matmul(bk[:, :], k, vbd[0:r, h, 4 * q:4 * q + 4, :],
                                                    start=True, stop=True)
                    else:
                        last = nc.tensor.matmul(S1[:, h * P:(h + 1) * P], k, vd[:, b, h * P:(h + 1) * P],
                                                start=True, stop=True)
                last.then_inc(b_o, 1)

            def tr8(src, banks, r):
                for k in range(KT):
                    last = nc.tensor.transpose(banks[k // 4][:, (k % 4) * P:(k % 4) * P + r],
                                               src[0:r, k * P:(k + 1) * P], eye[0:r, 0:r])
                return last

            def o_Tm(L, s):
                alone(pe, o_ms, L * STEPS + s.v + 1)
                tr8(msc, (TK, S0), s.rows).then_inc(o_tm, 1)

            def h_T(L, s):
                n = hn(L, s)
                if not (s.sample and isinstance(L, int) and L < 0):
                    pe.wait_ge(h_lo, n)
                alone(pe, h_xn, n + 1)
                tr8(xn, XX, s.rows).then_inc(h_t, 1)

            def step2(ph, L, s, f):
                for p in range(2):
                    for half in range(2):
                        proj(ph, L, s, p, half)
                        for work in f[2 * p + half]:
                            work()

            def a_step(L, s, f):
                proj("A", L, s, 0, 0)
                f[0]()
                proj("A", L, s, 0, 1)
                f[1]()
                proj("A", L, s, 1, 0)
                proj("A", L, s, 1, 1)
                f[2]()
                proj("A", L, s, 2, 0)
                f[3]()
                proj("A", L, s, 2, 1)
                f[4]()

            def a_work(L, s, old=True):
                def f0():
                    if old:
                        a_PT(L, s - 2, 1)
                    a_T(L, s - 1)

                def f1():
                    if old:
                        a_PV(L, s - 2, 1)
                    a_S(L, s - 1, 0)

                def f2():
                    if (s - 1).sample:
                        cached_keys(1).then_inc(s_ct, 1)

                def f3():
                    a_PT(L, s - 1, 0)
                    a_S(L, s - 1, 1)

                def f4():
                    a_PV(L, s - 1, 0)
                return [f0, f1, f2, f3, f4]

            def b_work(ph, L, s):
                return [[lambda: b_T(ph, L, s - 1)], [lambda: b_ST(ph, L, s - 1)],
                        [lambda: b_OS(ph, L, s - 1)], []]

            pe.wait_ge(c_ld, CONST_LOADS * 16)
            for c in range(2):
                h_T(-1, Step(c))
            with pe.Fori(0, (STEPS - 3) // 2) as i:
                h_T(-1, Step(2, i))
                h_T(-1, Step(3, i))
            h_T(-1, Step(STEPS - 1))
            with pe.Fori(0, DEPTH) as L:
                E = Step(STEPS - 1)
                pe.wait_ge(h_lo, (L + 1) * STEPS)
                pe.wait_ge(w_rd, wn(L, "A") + 1)
                nop = [lambda: None] * 5
                a_step(L, Step(0), nop)
                a_step(L, Step(1), a_work(L, Step(1), False))
                a_step(L, Step(2), a_work(L, Step(2)))
                with pe.Fori(0, (STEPS - 3) // 2) as i:
                    for c in (3, 4):
                        a_step(L, Step(c, i), a_work(L, Step(c, i)))

                pe.wait_ge(w_rd, wn(L, "B0") + 1)
                step2("B0", L, Step(0), [
                    [lambda: a_PT(L, E - 1, 1), lambda: a_T(L, E)],
                    [lambda: a_PV(L, E - 1, 1), lambda: a_S(L, E, 0)],
                    [],
                    [lambda: a_PT(L, E, 0), lambda: a_S(L, E, 1)]])
                step2("B0", L, Step(1), [
                    [lambda: a_PV(L, E, 0), lambda: b_T("B0", L, Step(0))],
                    [lambda: a_PT(L, E, 1), lambda: b_ST("B0", L, Step(0))],
                    [lambda: a_PV(L, E, 1)],
                    [lambda: b_OS("B0", L, Step(0))]])
                for ph, lo in (("B0", 2), ("B1", 1)):
                    if ph == "B1":
                        pe.wait_ge(w_rd, wn(L, "B1") + 1)
                        step2("B1", L, Step(0), b_work("B0", L, E + 1))
                    for c in range(lo, 3):
                        step2(ph, L, Step(c), b_work(ph, L, Step(c)))
                    with pe.Fori(0, (STEPS - 3) // 2) as i:
                        for c in (3, 4):
                            step2(ph, L, Step(c, i), b_work(ph, L, Step(c, i)))
    
                pe.wait_ge(w_rd, wn(L, "O") + 1)
                o_Tm(L, Step(0))
                step2("O", L, Step(0), [
                    [lambda: b_T("B1", L, E)], [lambda: b_ST("B1", L, E)],
                    [lambda: b_OS("B1", L, E)], [lambda: o_Tm(L, Step(1))]])
                def o_work(s):
                    return [[lambda: o_Tm(L, s + 1)], [], [lambda: h_T(L, s - 1)], []]
                for c in (1, 2):
                    step2("O", L, Step(c), o_work(Step(c)))
                with pe.Fori(0, (STEPS - 5) // 2) as i:
                    for c in (3, 4):
                        step2("O", L, Step(c, i), o_work(Step(c, i)))
                step2("O", L, E - 1, o_work(E - 1))
                step2("O", L, E, [[], [], [lambda: h_T(L, E - 1)], []])
                h_T(L, E)

        @block.vector
        def _(v):
            V = nc.vector

            def rsqrt(ch, x, y, t):
                ch(V.tensor_scalar(y.bitcast(I32), x.bitcast(I32), 1, None, ALU.logical_shift_right))
                V.tensor_scalar(x, x, -0.5, None, ALU.mult)
                ch(V.tensor_scalar(y.bitcast(I32), y.bitcast(I32), -1.0, MAGIC, ALU.mult, ALU.add))
                for _ in range(NEWTON):
                    ch(V.tensor_tensor(t, y, y, ALU.mult))
                    ch(V.tensor_tensor(t, t, x, ALU.mult))
                    ch(V.scalar_tensor_tensor(out=y, in0=t, scalar=1.5, in1=y, op0=ALU.add, op1=ALU.mult))

            def bc(col, n):
                return col.broadcast_to([col.shape[0], n])

            def w_absmax(L, kind, half):
                v.wait_ge(w_ld[half], 64 * (wn(L, kind) + 3 + 2 * L))
                for k in range(4 * half, 4 * half + 4):
                    last = V.tensor_reduce(w_mx[:, k:k + 1], raw(kind, k), AX.X, ALU.max,
                                           apply_absolute_value=True)
                if half == 1:
                    ch = Chain(v, ch_wm, 2, wn(L, kind))
                    ch(last)
                    ch(V.tensor_tensor(w_mx[:, :], w_mx[:, :], ones[:, :] if kind == "O" else g_cur[:, :],
                                       ALU.mult))
                    V.tensor_reduce(w_m1[:, :], w_mx[:, :], AX.X, ALU.max,
                                    apply_absolute_value=True).then_inc(w_max, 1)
                    ch.end()

            def w_scale(L, kind):
                ch = Chain(v, ch_ws, 4, wn(L, kind))
                v.wait_ge(w_all, wn(L, kind) + 1)
                ch(V.tensor_scalar(w_q[:, :], w_am[:, :], TOP, TINY, ALU.mult, ALU.max))
                ch(V.reciprocal(w_s[:, :], w_q[:, :]))
                V.tensor_scalar(w_gs[:, :], ones[:, :] if kind == "O" else g_cur[:, :], w_s[:, 0:1], None,
                                ALU.mult).then_inc(w_sc, 1)
                c = cs[kind]
                ch(V.tensor_scalar(c[:, 0:1], w_q[:, :], 1.0 if kind == "O" else 1.0 / H_SCALE, None, ALU.mult))
                if kind[0] == "B":
                    h = 2 * hb(kind)
                    V.tensor_scalar(c[:, 2:4], t_cols[:, 8 + h:10 + h], c[:, 0:1], None, ALU.mult)
                    V.tensor_scalar(c[0:NS, 4:6], t_cols[0:NS, 20 + h:22 + h], c[0:NS, 0:1], None, ALU.mult)
                V.tensor_scalar(c[:, 1:2], c[:, 0:1], 0.5, None, ALU.mult).then_inc(ch_ws, 1)
                ch.end(1)
                alone(v, ch_ws, (wn(L, kind) + 1) * ch.links)

            def w_gain(layer):
                src = g_all[:, layer, :] if isinstance(layer, int) else \
                    g_all[:, bass.ds(layer, 1), :].rearrange("p o k -> p (o k)")
                return V.tensor_copy(g_cur[:, :], src)

            def a_land_q(L, s):
                r, b = s.rows, s.par
                v.wait_ge(act_piece, apiece("A", L, s, 0) + 1)
                q = land[0:r, b, 0:A_W].rearrange("p (h d) -> p h d", d=A_DIM)
                src = bank("A", s, 0)[0:r, 0:A_W].rearrange("p (h d) -> p h d", d=A_DIM)
                g = qk_g[0:r, 0, :].unsqueeze(1).broadcast_to([r, A_HEADS, A_DIM])
                V.scalar_tensor_tensor(out=q, in0=src, scalar=cs["A"][0:r, 0:1], in1=g, op0=ALU.mult,
                                       op1=ALU.mult).then_inc(dve_piece, 1)
                V.tensor_reduce(ss[0:r, 0:8], sq[0:r, 0:A_W].rearrange("p (h d) -> p h d", d=A_DIM),
                                AX.X, ALU.add)

            def a_land_k(L, s):
                r, b = s.rows, s.par
                ch = Chain(v, ch_an, 4 + RSQRT_LINKS, an(L, s))
                v.wait_ge(act_piece, apiece("A", L, s, 1) + 1)
                k = land[0:r, b, A_W:A_W + KV_W].rearrange("p (h d) -> p h d", d=A_DIM)
                src = bank("A", s, 1)[0:r, 0:KV_W].rearrange("p (h d) -> p h d", d=A_DIM)
                g = qk_g[0:r, 1, :].unsqueeze(1).broadcast_to([r, A_KV, A_DIM])
                V.scalar_tensor_tensor(out=k, in0=src, scalar=cs["A"][0:r, 0:1], in1=g, op0=ALU.mult,
                                       op1=ALU.mult).then_inc(dve_piece, 1)
                ch(V.tensor_reduce(ss[0:r, 8:10], sq[0:r, A_W:A_W + KV_W].rearrange("p (h d) -> p h d", d=A_DIM),
                                   AX.X, ALU.add))
                ch(V.tensor_scalar(ss[0:r, :], ss[0:r, :], 1.0 / A_DIM, EPS, ALU.mult, ALU.add))
                y = rs[0:r, b, :]
                rsqrt(ch, ss[0:r, :], y, rt[0:r, :])
                h0 = 0 if s.sample else A_HEADS
                nh = A_HEADS + A_KV - h0
                x = land[0:r, b, h0 * A_DIM:(A_HEADS + A_KV) * A_DIM].rearrange("p (h d) -> p h d", d=A_DIM)
                ch(V.tensor_tensor(x, x, y[:, h0:].unsqueeze(2).broadcast_to([r, nh, A_DIM]), ALU.mult))
                V.tensor_scalar(y[:, 0:8], y[:, 0:8], A_DIM ** -0.5, None, ALU.mult)
                tab = t_ras[0:r, :, :] if s.sample else (
                    t_rap[:, s.tile, :, :] if s.fixed else
                    t_rap[:, bass.ds(s.tile, 1), :, :].rearrange("p o c d -> p (o c) d"))
                n, half = A_HEADS + A_KV, ROT // 2
                x = land[0:r, b, 0:n * A_DIM].rearrange("p (h d) -> p h d", d=A_DIM)
                xa, xb = x[:, :, 0:half], x[:, :, half:ROT]
                cos = tab[:, 0, :].unsqueeze(1).broadcast_to([r, n, half])
                sin = tab[:, 1, :].unsqueeze(1).broadcast_to([r, n, half])
                V.tensor_tensor(rp1[0:r, :, 0, :], xa, cos, ALU.mult)
                V.tensor_tensor(rp1[0:r, :, 1, :], xb, cos, ALU.mult)
                V.tensor_tensor(rp2[0:r, :, 0, :], xa, sin, ALU.mult)
                ch(V.tensor_tensor(rp2[0:r, :, 1, :], xb, sin, ALU.mult))
                V.tensor_tensor(xa, rp1[0:r, :, 0, :], rp2[0:r, :, 1, :], ALU.subtract)
                V.tensor_tensor(xb, rp1[0:r, :, 1, :], rp2[0:r, :, 0, :], ALU.add).then_inc(a_qk, 1)
                ch.end()

            def gate(ph, L, s, p, n, col):
                r, b = s.rows, lpar(ph, s)
                v.wait_ge(act_piece, apiece(ph, L, s, 2) + 1)
                th = land[0:r, b, col:col + n]
                V.scalar_tensor_tensor(out=th, in0=th, scalar=1.0, in1=bank(ph, s, p)[0:r, 512 - n:512],
                                       op0=ALU.add, op1=ALU.mult).then_inc(dve_piece, 1)

            def a_vcopy(L, s):
                if not s.sample:
                    V.tensor_copy(vr[:, s.par, :], land[:, s.par, A_W + KV_W:A_W + 2 * KV_W])

            def a_softmax(L, s, g):
                n = 2 * an(L, s) + g
                ch = Chain(v, ch_asm, 3, n)
                alone(v, a_s, n + 1)
                if s.sample:
                    parts = ((S0[:, :], 0, 512), (S1[:, :], 512, 512), (TK[:, 0:NS], KEYS, NS))
                    for q, (src, o, w) in enumerate(parts):
                        last = V.tensor_tensor_reduce(
                            out=prob[:, o:o + w], in0=src, in1=t_ms[:, o:o + w].bitcast(BF16), scale=1.0, scalar=-3e38,
                            op0=ALU.add, op1=ALU.max, accum_out=mr[:, g, q:q + 1])
                    ch(last)
                    ch(V.tensor_reduce(rt[:, 0:1], mr[:, g, 0:3], AX.X, ALU.max))
                    ch(V.scalar_tensor_tensor(out=nm[:, g, 0:1], in0=rt[:, 0:1], scalar=-(A_DIM ** -0.5),
                                              in1=nsks[:, g:g + 1], op0=ALU.mult, op1=ALU.min))
                    V.tensor_tensor(sd[:, g, 0:1], nm[:, g, 0:1], sks[:, g:g + 1], ALU.add).then_inc(a_sm, 1)
                else:
                    m = t_ma[:, 2 if s.first else s.par, :].bitcast(BF16)
                    for h in range(A_GROUP):
                        last = V.tensor_tensor_reduce(
                            out=prob[:, h * 256:(h + 1) * 256], in0=SS[h // 2][:, (h % 2) * 256:(h % 2) * 256 + 256],
                            in1=m, scale=1.0, scalar=-3e38, op0=ALU.add, op1=ALU.max,
                            accum_out=mr[:, g, h:h + 1])
                    ch(last)
                    gs = slice(g * A_GROUP, (g + 1) * A_GROUP)
                    ch(V.scalar_tensor_tensor(out=nm[:, g, :], in0=mr[:, g, :], scalar=-1.0,
                                              in1=rs[:, s.par, g:A_HEADS:A_KV], op0=ALU.mult, op1=ALU.mult))
                    ch(V.tensor_tensor(nm[:, g, :], nm[:, g, :], nsk[:, gs], ALU.min))
                    V.tensor_tensor(sd[:, g, :], nm[:, g, :], sk[:, gs], ALU.add).then_inc(a_sm, 1)
                ch.end()

            def a_mix(L, s, g):
                n, b = 2 * an(L, s) + g, s.par
                ch = Chain(v, ch_amx, 3, n)
                w = 1 if s.sample else A_GROUP
                v.wait_ge(a_ex, n + 1)
                ch(V.tensor_tensor(rr[:, g, 0:w], rsum[:, g, 0:w], es[:, g, 0:w], ALU.add))
                ch(V.reciprocal(rr[:, g, 0:w], rr[:, g, 0:w]))
                ch(V.tensor_scalar(rr[:, g, 0:w], rr[:, g, 0:w], cs["A"][:, 1:2], None, ALU.mult))
                v.wait_ge(a_pv, n + 1)
                if g == 0:
                    v.wait_ge(mix_out[b], 16 * mix_count("A", L, s))
                th0 = A_W + 2 * KV_W + g * A_GROUP * A_DIM
                if s.sample:
                    tmp = kts[0:NS, 0:A_GROUP * A_DIM]
                    for h in range(A_GROUP):
                        q = slice(h * NS, (h + 1) * NS)
                        last = V.tensor_scalar(tmp[:, h * A_DIM:(h + 1) * A_DIM], OB[q, 0:A_DIM],
                                               rr[q, g, 0:1], None, ALU.mult)
                    last.then_inc(ch_ams, 1)
                    v.wait_ge(ch_ams, 2 * L + g + 1)
                    V.tensor_tensor(mix[0:NS, b, g * 256:(g + 1) * 256], tmp, land[0:NS, b, th0:th0 + 256],
                                    ALU.mult).then_inc(a_mx, 1)
                else:
                    for h in range(A_GROUP):
                        o = h * A_DIM
                        last = V.scalar_tensor_tensor(
                            out=mix[:, b, g * 256 + o:g * 256 + o + A_DIM], in0=OB[:, o:o + A_DIM],
                            scalar=rr[:, g, h:h + 1], in1=land[:, b, th0 + o:th0 + o + A_DIM],
                            op0=ALU.mult, op1=ALU.mult)
                    last.then_inc(a_mx, 1)
                ch.end()

            def b_rope(ph, L, s):
                r, b = s.rows, lpar(ph, s)
                v.wait_ge(pe_piece, piece(ph, L, s, 0) + 1)
                tab = t_rbs[0:r, :, :] if s.sample else (
                    t_rbp[:, s.tile, :, :] if s.fixed else
                    t_rbp[:, bass.ds(s.tile, 1), :, :].rearrange("p o c d -> p (o c) d"))
                src = bank(ph, s, 0)[0:r, :].rearrange("p (g d) -> p g d", d=DK // 2)
                for out, i in ((t1, 0), (t2, 1)):
                    last = V.scalar_tensor_tensor(
                        out=out[0:r, :].rearrange("p (g d) -> p g d", d=DK // 2), in0=src,
                        scalar=cs[ph][0:r, 0:1], in1=tab[:, i, :].unsqueeze(1).broadcast_to([r, 8, DK // 2]),
                        op0=ALU.mult, op1=ALU.mult)
                last.then_inc(dve_piece, 1)
                v.wait_ge(dve_piece, piece(ph, L, s, 0) + 2)
                a, c = (t[0:r, :].rearrange("p (g c d) -> p g c d", c=2, d=DK // 2) for t in (t1, t2))
                o = land[0:r, b, 0:512].rearrange("p (g c d) -> p g c d", c=2, d=DK // 2)
                V.tensor_tensor(o[:, :, 0, :], a[:, :, 0, :], c[:, :, 1, :], ALU.subtract)
                V.tensor_tensor(o[:, :, 1, :], a[:, :, 1, :], c[:, :, 0, :], ALU.add).then_inc(b_qk, 1)

            def b_decay(ph, L, s):
                v.wait_ge(b_st, bn(ph, L, s) + 1)
                h = 2 * hb(ph)
                if s.sample:
                    out = stm[0:NS, 0:2 * NS].rearrange("p (h n) -> p h n", h=2)
                    src = S0[0:NS, 0:2 * NS].rearrange("p (h n) -> p h n", h=2)
                    V.tensor_tensor(out, src, t_decs[:, h:h + 2, :], ALU.mult).then_inc(b_dm, 1)
                else:
                    V.tensor_tensor(stm, S0[:, 0:256], t_dec[:, h:h + 2, :].rearrange("p h n -> p (h n)"),
                                    ALU.mult).then_inc(b_dm, 1)

            def b_vbd(ph, L, s):
                v.wait_ge(act_piece, apiece(ph, L, s, 1) + 1)
                b = lpar(ph, s)
                for h in range(2):
                    x = vd[0:NS, b, h * P:(h + 1) * P].unsqueeze(1).broadcast_to([NS, DEC_BATCH, P])
                    m = t_cols[0:NS, 24:32].unsqueeze(2).broadcast_to([NS, DEC_BATCH, P])
                    last = V.tensor_tensor(vbd[0:NS, h, :, :], x, m, ALU.mult)
                last.then_inc(b_vb, 1)

            def b_state(ph, L, s):
                v.wait_ge(b_o, bn(ph, L, s) + 1)
                st, h0 = state[hb(ph)], 2 * hb(ph)
                if s.sample:
                    for h in range(2):
                        for q, bk in enumerate(((S1, X0), (X1, S0))[h]):
                            x = stS[:, h, 4 * q:4 * q + 4, :]
                            V.scalar_tensor_tensor(out=x, in0=x, scalar=lam(h0 + h) ** DEC_SEQ,
                                                   in1=bk[:, :].rearrange("p (b v) -> p b v", v=DV),
                                                   op0=ALU.mult, op1=ALU.add)
                    v.wait_ge(st_out, (L + 1) * 64)
                    V.memset(st, 0.0).then_inc(b_su, 1)
                else:
                    for h in range(2):
                        x = st[:, h * P:(h + 1) * P]
                        last = V.scalar_tensor_tensor(out=x, in0=x, scalar=lam(h0 + h) ** P,
                                                      in1=S1[:, h * P:(h + 1) * P], op0=ALU.mult, op1=ALU.add)
                    last.then_inc(b_su, 1)

            def b_mix(ph, L, s):
                r, n, b = s.rows, bn(ph, L, s), lpar(ph, s)
                ch = Chain(v, ch_bo, 4 + RSQRT_LINKS, n)
                h0, cc = 2 * hb(ph), 12 if s.sample else 0
                v.wait_ge(b_sq, n + 1)
                ch(V.tensor_tensor(oms[0:r, :], oss[0:r, :], t_cols[0:r, cc + h0:cc + h0 + 2], ALU.mult))
                ch(V.tensor_scalar(oms[0:r, :], oms[0:r, :], EPS, None, ALU.add))
                rsqrt(ch, oms[0:r, :], oy[0:r, :], ot[0:r, :])
                ch(V.tensor_tensor(oy[0:r, :], oy[0:r, :], t_cols[0:r, cc + 4 + h0:cc + 6 + h0], ALU.mult))
                ch(V.tensor_scalar(oy[0:r, :], oy[0:r, :], cs[ph][0:r, 1:2], None, ALU.mult))
                v.wait_ge(mix_out[b], 16 * mix_count(ph, L, s))
                for h in range(2):
                    c = slice(h * P, (h + 1) * P)
                    last = V.scalar_tensor_tensor(out=mix[0:r, b, c], in0=OB[0:r, c], scalar=oy[0:r, h:h + 1],
                                                  in1=land[0:r, b, 768 + h * P:768 + (h + 1) * P],
                                                  op0=ALU.mult, op1=ALU.mult)
                last.then_inc(b_mx, 1)
                ch.end()

            def o_scale(L, s):
                r, b = s.rows, s.par
                ch = Chain(v, ch_om, 2, L * STEPS + s.v)
                v.wait_ge(mx_ld[b], 16 * (L * (9 - b) + s.half + 1))
                ch(V.tensor_reduce(mq[0:r, :], mxt[0:r, b, :], AX.X, ALU.max, apply_absolute_value=True))
                ch(V.tensor_scalar(mqq[0:r, b:b + 1], mq[0:r, :], TOP, TINY, ALU.mult, ALU.max))
                V.reciprocal(minv[0:r, b:b + 1], mqq[0:r, b:b + 1]).then_inc(o_sc, 1)
                ch.end()

            def o_unscale(L, s):
                r, b = s.rows, s.par
                ch = Chain(v, ch_ou, 1, L * STEPS + s.v)
                ch(V.tensor_scalar(mdd[0:r, b:b + 1], mqq[0:r, b:b + 1], cs["O"][0:r, 0:1], None, ALU.mult))
                ch.end()

            def lo(ready, n, banks, r, dst):
                for q, bk in enumerate(banks):
                    v.wait_ge(ready, n + q + 1)
                    src = bk[:, :].rearrange("p (k t) -> p k t", t=P)[:, :, 0:r]
                    last = V.tensor_tensor(dst(1, q), src, dst(0, q), ALU.subtract)
                return last

            def o_mlo(L, s):
                m = mT[s.par]
                lo(o_hi, 2 * (L * STEPS + s.v), (TK, S0), s.rows,
                   lambda e, q: m[:, 4 * q:4 * q + 4, e, 0:s.rows]).then_inc(o_lo, 1)

            def h_lo_part(L, s):
                lo(h_hi, 2 * hn(L, s), XX, s.rows,
                   lambda e, q: hT[:, e, 4 * q:4 * q + 4, hcols(s)]).then_inc(h_lo, 1)

            def o_add(L, s, p):
                r, b = s.rows, s.par
                v.wait_ge(pe_piece, piece("O", L, s, p) + 1)
                if p == 0:
                    v.wait_ge(x_ld[b], 16 * ((L + 1) * (9 - b) + s.half + 1))
                x = xt_[0:r, b, p * 512:(p + 1) * 512]
                V.scalar_tensor_tensor(out=x, in0=bank("O", s, p)[0:r, :], scalar=mdd[0:r, b:b + 1], in1=x,
                                       op0=ALU.mult, op1=ALU.add).then_inc(dve_piece, 1)

            def h_rstd(L, s):
                r, b = s.rows, s.par
                ch = Chain(v, ch_h, 1 + RSQRT_LINKS, hn(L, s))
                v.wait_ge(h_sq, hn(L, s) + 1)
                ch(V.tensor_scalar(xms[0:r, :], xss[0:r, :], 1.0 / D_MODEL, EPS, ALU.mult, ALU.add))
                y = xy[0:r, b:b + 1]
                rsqrt(ch, xms[0:r, :], y, xt[0:r, :])
                V.tensor_scalar(y, y, H_SCALE, None, ALU.mult).then_inc(h_rs, 1)
                ch.end()

            E = Step(STEPS - 1)
            v.sem_inc(dve_piece, 1)
            V.memset(ones[:, :], 1.0)
            v.wait_ge(c_ld, CONST_LOADS * 16)
            w_gain(0).then_inc(ch_l, 1)
            v.wait_ge(ch_l, 1)

            def h_part(L, s):
                h_rstd(L, s)
                h_lo_part(L, s)

            for c in range(2):
                h_part(-1, Step(c))
            with v.Fori(0, 3) as i:
                for c in (2, 3):
                    h_part(-1, Step(c, i))
            w_absmax(0, "A", 0)
            w_absmax(0, "A", 1)
            w_scale(0, "A")
            with v.Fori(0, 4) as i:
                for c in (8, 9):
                    h_part(-1, Step(c, i))
            h_part(-1, E)

            with v.Fori(0, DEPTH) as L:
                V.tensor_copy(qk_g[:, :, :], qk_all[:, bass.ds(L, 1), :, :].rearrange("p o c d -> p (o c) d"))
                V.tensor_copy(sk[:, :], sk_all[:, bass.ds(L, 1), :].rearrange("p o k -> p (o k)"))
                V.tensor_scalar(nsk[:, :], sk_all[:, bass.ds(L, 1), :].rearrange("p o k -> p (o k)"), -1.0,
                                None, ALU.mult)
                V.tensor_copy(sks[:, :], sks_all[:, bass.ds(L, 1), :].rearrange("p o k -> p (o k)"))
                V.tensor_scalar(nsks[:, :], sks_all[:, bass.ds(L, 1), :].rearrange("p o k -> p (o k)"), -1.0,
                                None, ALU.mult).then_inc(ch_l, 1)
                v.wait_ge(ch_l, L * 2 + 2)

                def a_step(s, weights=None):
                    a_land_q(L, s)
                    if not (s.fixed and s.c < 2):
                        a_mix(L, s - 2, 1)
                    if not s.sample:
                        a_vcopy(L, s - 1)
                        a_softmax(L, s - 1, 0)
                    a_land_k(L, s)
                    if not s.sample:
                        a_softmax(L, s - 1, 1)
                    gate("A", L, s, 2, A_W, A_W + 2 * KV_W)
                    if not s.sample:
                        a_mix(L, s - 1, 0)

                for c in range(5):
                    a_step(Step(c))
                    if c in (2, 3):
                        w_absmax(L, "B0", c - 2)
                    if c == 4:
                        w_scale(L, "B0")
                with v.Fori(0, 6) as i:
                    for c in (5, 6):
                        a_step(Step(c, i))

                s = Step(0)
                a_mix(L, E - 1, 1)
                a_vcopy(L, E)
                a_softmax(L, E, 0)
                V.memset(r1[:, 2048:2048 + 2 * 288], 0.0)
                b_rope("B0", L, s)
                a_softmax(L, E, 1)
                gate("B0", L, s, 1, 256, 768)
                a_mix(L, E, 0)
                s = Step(1)
                b_rope("B0", L, s)
                b_decay("B0", L, Step(0))
                a_mix(L, E, 1)
                b_vbd("B0", L, Step(0))
                gate("B0", L, s, 1, 256, 768)
                b_state("B0", L, Step(0))
                b_mix("B0", L, Step(0))

                def b_old(ph, s):
                    b_state(ph, L, s)
                    b_mix(ph, L, s)

                def b_step(ph, s):
                    if s.fixed and s.c == 1:
                        b_vbd(ph, L, s - 1)
                    b_decay(ph, L, s - 1)
                    b_rope(ph, L, s)
                    b_old(ph, s - 1)
                    gate(ph, L, s, 1, 256, 768)

                for ph, lo_c, nxt in (("B0", 2, "B1"), ("B1", 1, "O")):
                    if ph == "B1":
                        b_decay("B0", L, E)
                        b_rope("B1", L, Step(0))
                        b_old("B0", E)
                        gate("B1", L, Step(0), 1, 256, 768)
                    for c in range(lo_c, 5):
                        b_step(ph, Step(c))
                        if c in (2, 3):
                            w_absmax(L, nxt, c - 2)
                        if c == 4:
                            w_scale(L, nxt)
                    with v.Fori(0, 6) as i:
                        for c in (5, 6):
                            b_step(ph, Step(c, i))

                o_scale(L, Step(0))
                o_unscale(L, Step(0))
                o_mlo(L, Step(0))
                o_scale(L, Step(1))
                o_unscale(L, Step(1))
                b_decay("B1", L, E)
                o_add(L, Step(0), 0)
                b_old("B1", E)
                o_add(L, Step(0), 1)
                o_mlo(L, Step(1))
                o_scale(L, Step(2))

                def o_step(s):
                    h_rstd(L, s - 1)
                    if not (s.fixed and s.c == STEPS - 1):
                        v.wait_ge(dve_piece, piece("O", L, s - 1, 1) + 2)
                        o_unscale(L, s + 1)
                        o_mlo(L, s + 1)
                    if not (s.fixed and s.c >= STEPS - 2):
                        o_scale(L, s + 2)
                    o_add(L, s, 0)
                    h_lo_part(L, s - 1)
                    o_add(L, s, 1)

                for c in range(1, 5):
                    o_step(Step(c))
                    if c == 2:
                        w_gain((L + 1) % DEPTH).then_inc(ch_l, 1)
                        v.wait_ge(ch_l, L * 2 + 3)
                        w_absmax(L + 1, "A", 0)
                    if c == 3:
                        w_absmax(L + 1, "A", 1)
                    if c == 4:
                        w_scale(L + 1, "A")
                with v.Fori(0, 5) as i:
                    for c in (5, 6):
                        o_step(Step(c, i))
                o_step(E - 1)
                o_step(E)
                h_part(L, E)

        @block.scalar
        def _(act):
            A = nc.scalar

            def a_q(L, s):
                r = s.rows
                act.wait_ge(pe_piece, piece("A", L, s, 0) + 1)
                A.activation(sq[0:r, 0:A_W], bank("A", s, 0)[0:r, :], ACT.Square,
                             scale=cs["A"][0:r, 0:1]).then_inc(act_piece, 1)

            def a_kv(L, s):
                r, b, c = s.rows, s.par, cs["A"]
                act.wait_ge(pe_piece, piece("A", L, s, 1) + 1)
                if s.fixed and s.c == 2:
                    act.wait_ge(kvs_out, (L + 1) * 256)
                src = bank("A", s, 1)
                A.activation(sq[0:r, A_W:A_W + KV_W], src[0:r, 0:KV_W], ACT.Square, scale=c[0:r, 0:1])
                A.activation(land[0:r, b, A_W + KV_W:A_W + 2 * KV_W], src[0:r, KV_W:2 * KV_W], ACT.Copy,
                             scale=c[0:r, 0:1]).then_inc(act_piece, 1)

            def a_tanh(L, s):
                r = s.rows
                act.wait_ge(pe_piece, piece("A", L, s, 2) + 1)
                A.activation(land[0:r, s.par, A_W + 2 * KV_W:], bank("A", s, 2)[0:r, :], ACT.Tanh,
                             scale=cs["A"][0:r, 1:2]).then_inc(act_piece, 1)

            def a_tout(L, s):
                act.wait_ge(a_tk, an(L, s) + 1)
                if s.sample:
                    A.activation(qT[0:A_DIM, 0:A_HEADS * NS], TK[0:A_DIM, 0:A_HEADS * NS], ACT.Copy)
                    A.activation(knew[0:A_DIM, :, :].rearrange("p g n -> p (g n)"),
                                 TK[0:A_DIM, A_HEADS * NS:(A_HEADS + A_KV) * NS], ACT.Copy)
                    last = cached_keys_out()
                else:
                    A.activation(qT[:, :], TK[:, :], ACT.Copy)
                    last = A.activation(kT[:, s.par * P:(s.par + 1) * P], S0[:, 0:P], ACT.Copy)
                last.then_inc(a_te, 1)

            def cached_keys_out():
                for q in range(2):
                    last = A.activation(kts[0:A_DIM, q * 512:(q + 1) * 512], XX[q][0:A_DIM, :], ACT.Copy)
                return last

            def a_exp(L, s, g):
                act.wait_ge(a_sm, 2 * an(L, s) + g + 1)
                if s.sample:
                    A.activation(prob[:, :], prob[:, :], ACT.Exp, scale=A_DIM ** -0.5, bias=nm[:, g, 0:1],
                                 accum_out=rsum[:, g, 0:1])
                else:
                    for h in range(A_GROUP):
                        x = prob[:, h * 256:(h + 1) * 256]
                        q = h * A_KV + g
                        A.activation(x, x, ACT.Exp, scale=rs[:, s.par, q:q + 1], bias=nm[:, g, h:h + 1],
                                     accum_out=rsum[:, g, h:h + 1])
                w = 1 if s.sample else A_GROUP
                A.activation(es[:, g, 0:w], sd[:, g, 0:w], ACT.Exp).then_inc(a_ex, 1)

            def a_pout(L, s, g):
                act.wait_ge(a_pt, 2 * an(L, s) + g + 1)
                for q in range(2):
                    last = A.activation(pT[:, q * 512:(q + 1) * 512], XX[q][:, :], ACT.Copy)
                if s.sample:
                    last = A.activation(pT[0:NS, KEYS:KEYS + P], TK[0:NS, P:2 * P], ACT.Copy)
                last.then_inc(a_po, 1)

            def b_vg(ph, L, s):
                r, b, c = s.rows, lpar(ph, s), cs[ph]
                act.wait_ge(pe_piece, piece(ph, L, s, 1) + 1)
                if ph == "B0" and s.fixed and s.c == 1:
                    act.wait_ge(kv_out, (L + 1) * 32)
                src = bank(ph, s, 1)
                A.activation(land[0:r, b, 512:768], src[0:r, 0:256], ACT.Copy, scale=c[0:r, 0:1])
                k = 4 if s.sample else 2
                for h in range(2):
                    A.activation(vd[0:r, b, h * P:(h + 1) * P], src[0:r, h * P:(h + 1) * P], ACT.Copy,
                                 scale=c[0:r, k + h:k + h + 1])
                A.activation(land[0:r, b, 768:1024], src[0:r, 256:512], ACT.Tanh,
                             scale=c[0:r, 1:2]).then_inc(act_piece, 1)

            def b_tout(ph, L, s):
                act.wait_ge(b_tk, bn(ph, L, s) + 1)
                if s.sample:
                    A.activation(qkT[:, 0:4 * NS], TK[:, 0:4 * NS], ACT.Copy)
                    for h in range(2):
                        last = A.activation(
                            qtm[:, h, :].rearrange("p (b x) -> p b x", x=NS + DEC_SEQ)[:, :, 0:DEC_SEQ],
                            TK[:, h * NS:(h + 1) * NS].rearrange("p (b x) -> p b x", x=DEC_SEQ), ACT.Copy)
                else:
                    last = A.activation(qkT[:, :], TK[:, :], ACT.Copy)
                last.then_inc(b_te, 1)

            def b_squares(ph, L, s):
                r = s.rows
                act.wait_ge(b_o, bn(ph, L, s) + 1)
                for h in range(2):
                    last = A.activation(osq[0:r, h * P:(h + 1) * P], OB[0:r, h * P:(h + 1) * P], ACT.Square,
                                        accum_out=oss[0:r, h:h + 1])
                last.then_inc(b_sq, 1)

            def o_mscale(L, s):
                r, b, n = s.rows, s.par, L * STEPS + s.v
                act.wait_ge(o_sc, n + 1)
                if not s.sample:
                    act.wait_ge(o_tm, n)
                A.activation(msc[0:r, :], mxt[0:r, b, :], ACT.Copy, scale=minv[0:r, b:b + 1]).then_inc(o_ms, 1)

            def hi(banks, r, dst, ready):
                for q, bk in enumerate(banks):
                    src = bk[:, :].rearrange("p (k t) -> p k t", t=P)[:, :, 0:r]
                    A.activation(dst(q), src, ACT.Copy).then_inc(ready, 1)

            def o_mhi(L, s):
                act.wait_ge(o_tm, L * STEPS + s.v + 1)
                m = mT[s.par]
                hi((TK, S0), s.rows, lambda q: m[:, 4 * q:4 * q + 4, 0, 0:s.rows], o_hi)

            def h_squares(L, s):
                r, b = s.rows, s.par
                if isinstance(L, int) and L < 0:
                    act.wait_ge(x_ld[b], 16 * (s.half + 1))
                else:
                    act.wait_ge(dve_piece, piece("O", L, s, 1) + 2)
                if not (s.sample and isinstance(L, int) and L < 0):
                    act.wait_ge(h_t, hn(L, s))
                A.activation(xn[0:r, :], xt_[0:r, b, :], ACT.Square, accum_out=xss[0:r, :]).then_inc(h_sq, 1)

            def h_norm(L, s):
                r, b = s.rows, s.par
                act.wait_ge(h_rs, hn(L, s) + 1)
                A.activation(xn[0:r, :], xt_[0:r, b, :], ACT.Copy, scale=xy[0:r, b:b + 1]).then_inc(h_xn, 1)

            def h_hi_part(L, s):
                act.wait_ge(h_t, hn(L, s) + 1)
                hi(XX, s.rows, lambda q: hT[:, 0, 4 * q:4 * q + 4, hcols(s)], h_hi)

            def h_part(L, s):
                h_squares(L, s)
                h_norm(L, s)
                h_hi_part(L, s)

            E = Step(STEPS - 1)
            act.wait_ge(init, 1)
            for c in range(2):
                h_part(-1, Step(c))
            with act.Fori(0, (STEPS - 3) // 2) as i:
                for c in (2, 3):
                    h_part(-1, Step(c, i))
            h_part(-1, E)
            with act.Fori(0, DEPTH) as L:
                def a_step(s):
                    tail, old = not s.sample, not (s.fixed and s.c < 2)
                    if old:
                        a_pout(L, s - 2, 1)
                    if tail:
                        a_tout(L, s - 1)
                    a_q(L, s)
                    if tail:
                        a_exp(L, s - 1, 0)
                    a_kv(L, s)
                    if tail:
                        if (s - 1).sample:
                            act.wait_ge(s_ct, L + 1)
                            cached_keys_out().then_inc(s_ce, 1)
                        a_pout(L, s - 1, 0)
                        a_exp(L, s - 1, 1)
                    a_tanh(L, s)

                for c in range(3):
                    a_step(Step(c))
                with act.Fori(0, (STEPS - 3) // 2) as i:
                    for c in (3, 4):
                        a_step(Step(c, i))
                a_pout(L, E - 1, 1)
                a_tout(L, E)
                a_exp(L, E, 0)
                a_pout(L, E, 0)
                b_vg("B0", L, Step(0))
                a_exp(L, E, 1)
                b_tout("B0", L, Step(0))
                a_pout(L, E, 1)
                b_vg("B0", L, Step(1))
                b_squares("B0", L, Step(0))

                def b_step(ph, s):
                    b_tout(ph, L, s - 1)
                    b_squares(ph, L, s - 1)
                    b_vg(ph, L, s)

                for ph, lo_c in (("B0", 2), ("B1", 1)):
                    if ph == "B1":
                        b_tout("B0", L, E)
                        b_squares("B0", L, E)
                        b_vg("B1", L, Step(0))
                    for c in range(lo_c, 3):
                        b_step(ph, Step(c))
                    with act.Fori(0, (STEPS - 3) // 2) as i:
                        for c in (3, 4):
                            b_step(ph, Step(c, i))
                o_mscale(L, Step(0))
                o_mhi(L, Step(0))
                b_tout("B1", L, E)
                b_squares("B1", L, E)
                o_mscale(L, Step(1))
                act.wait_ge(st_out, (L + 1) * 64 + 64)
                o_mhi(L, Step(1))
                o_mscale(L, Step(2))

                def o_step(s):
                    h_squares(L, s - 1)
                    if not (s.fixed and s.c == STEPS - 1):
                        o_mhi(L, s + 1)
                    h_norm(L, s - 1)
                    if not (s.fixed and s.c >= STEPS - 2):
                        o_mscale(L, s + 2)
                    h_hi_part(L, s - 1)

                for c in range(1, 3):
                    o_step(Step(c))
                with act.Fori(0, (STEPS - 5) // 2) as i:
                    for c in (3, 4):
                        o_step(Step(c, i))
                o_step(E - 1)
                o_step(E)
                h_part(L, E)

        @block.gpsimd
        def _(pool):
            G = nc.gpsimd
            win = w_in.rearrange("l (k p) n -> l p k n", p=P)
            wout = w_out.rearrange("l (k p) n -> l p k n", p=P)

            def load(L, kind, layer):
                def cols(k, c0, n):
                    src = wout if kind == "O" else win
                    if isinstance(layer, int):
                        return src[layer, :, k, c0:c0 + n]
                    return src[bass.ds(layer, 1), :, k, c0:c0 + n].rearrange("o p n -> (o p) n")

                for k in range(KT):
                    s = w_ld[k // 4]
                    if kind == "A":
                        for g in range(A_KV):
                            G.dma_start(raw(kind, k, 0).rearrange("p (h g d) -> p h g d", g=A_KV, d=A_DIM)[:, :, g, :],
                                        cols(k, g * 256, 256).rearrange("p (h d) -> p h d", d=A_DIM)).then_inc(s, 16)
                        G.dma_start(raw(kind, k)[:, A_W:], cols(k, A_W, N_A - A_W)).then_inc(s, 16)
                    elif kind == "O":
                        G.dma_start(raw(kind, k), cols(k, 0, WIDTH[kind])).then_inc(s, 16)
                    else:
                        src = win[:, :, k, N_A:IN_W].rearrange("l p (q n) -> l p q n", q=4)
                        o = hb(kind) * 2 * DK
                        G.dma_start(raw(kind, k).rearrange("p (q n) -> p q n", q=4),
                                    src[bass.ds(layer, 1), :, :, o:o + 2 * DK].rearrange("o p q n -> (o p) q n")
                                    ).then_inc(s, 16)

            def convert(L, kind, done):
                alone(pool, w_max, wn(L, kind) + 1)
                G.partition_all_reduce(w_am[:, :], w_m1[:, :], P, bass.bass_isa.ReduceOp.max).then_inc(w_all, 1)
                pool.wait_ge(w_sc, wn(L, kind) + 1)
                ch = Chain(pool, ch_wp, 1, done * 3)
                for k in range(KT):
                    for c, (c0, n) in enumerate(CH[kind]):
                        g = w_gs[:, k:k + 1].broadcast_to([P, n])
                        t = w_tmp[:, 0:n]
                        ch(G.tensor_tensor(t, raw(kind, k, c), g, ALU.mult))
                        ch(G.tensor_tensor(w16(kind, k, c, 0), t, ones[:, 0:1].broadcast_to([P, n]), ALU.mult))
                        ch(G.tensor_tensor(w16(kind, k, c, 1), t, w16(kind, k, c, 0), ALU.subtract))
                pool.sem_inc(w_rd, 1)

            chunks = {k: KT * len(CH[k]) for k in BLOCKS}
            load(0, "A", 0)
            G.memset(r2[:, :], 0.0).then_inc(init, 1)
            for p in range(2):
                pool.sem_inc(mix_out[p], 16)
            pool.sem_inc(st_out, 64)
            convert(0, "A", 0)
            with pool.Fori(0, DEPTH) as L:
                base = chunks["A"] + L * sum(chunks.values())
                for kind, after in (("B0", "A"), ("B1", "B0"), ("O", "B1"), ("A", "O")):
                    nl = L + 1 if kind == "A" else L
                    pool.wait_ge(dve_piece, L * PIECES + PIECE0[after] + 1)
                    load(nl, kind, (L + 1) % DEPTH if kind == "A" else L)
                    convert(nl, kind, base)
                    base = base + chunks[kind]

        @block.sync
        def _(sp):
            def xs(s, prompt, sample):
                return sample if s.sample else (
                    prompt[s.col:s.col + P, :] if s.fixed else prompt[bass.ds(s.col, P), :])

            def load_x(L, s, prompt, sample):
                sp.dma_start(xt_[0:s.rows, s.par, :], xs(s, prompt, sample)).then_inc(x_ld[s.par], 16)

            def mixed_rows(s):
                return slice(s.col, s.col + s.rows) if s.fixed else bass.ds(s.col, P)

            def store_mix(ph, L, s):
                p = lpar(ph, s)
                if ph == "A":
                    sp.wait_ge(a_mx, 2 * an(L, s) + 2)
                    c0, n = 0, A_W
                else:
                    sp.wait_ge(b_mx, bn(ph, L, s) + 1)
                    c0, n = A_W + hb(ph) * 256, 256
                sp.dma_start(mixed[mixed_rows(s), c0:c0 + n], mix[0:s.rows, p, 0:n]).then_inc(mix_out[p], 16)

            def load_mixed(L, s):
                p = s.par
                sp.wait_ge(mix_out[p], 16 * mix_count("B1", L, s) + 16)
                sp.wait_ge(mix_out[1 - p], 16 * (L * MIX_OUT[1 - p] + MIX_OUT0["B1"][1 - p]) + 16)
                sp.dma_start(mxt[0:s.rows, p, :], mixed[mixed_rows(s), :]).then_inc(mx_ld[p], 16)

            def load_states(ph, L):
                for h in range(2):
                    src = state_ret[bass.ds(L, 1), :, 2 * hb(ph) + h, :, :].rearrange("o b k v -> k (o b) v")
                    sp.dma_start(stS[:, h, :, :], src).then_inc(sts_ld, 16)

            xp, ys = x_prompt[0], y_p[0]
            xsm, ysm = x_sample.rearrange("b t d -> (b t) d"), y_s.rearrange("b t d -> (b t) d")
            load_x(-1, Step(0), xp, xsm)
            load_x(-1, Step(1), xp, xsm)
            loads = [(eye[:, :], ident), (t_cols[:, :], cols), (t_rap[:, :, :, :], rope_ap), (t_ras[:, :, :], rope_as),
                     (t_rbp[:, :, :, :], rope_bp), (t_rbs[:, :, :], rope_bs), (t_ma[:, :, :], mask_a),
                     (t_ms[:, :], mask_s), (t_dec[:, :, :], decay), (t_decs[:, :, :], decay_s)]
            for l in range(DEPTH):
                loads.append((g_all[:, l, :], norm_g[l].rearrange("(k p) -> p k", p=P)))
                loads.append((qk_all[:, l, 0, :], q_g[l:l + 1, :].broadcast_to([P, A_DIM])))
                loads.append((qk_all[:, l, 1, :], k_g[l:l + 1, :].broadcast_to([P, A_DIM])))
                loads.append((sk_all[:, l, :], sinks[l:l + 1, :].broadcast_to([P, A_HEADS])))
                for h in range(A_HEADS):
                    g, q = h // A_GROUP, h % A_GROUP
                    loads.append((sks_all[q * NS:(q + 1) * NS, l, g:g + 1],
                                  sinks[l:l + 1, h:h + 1].broadcast_to([NS, 1])))
            assert len(loads) == CONST_LOADS
            with nc.allow_non_contiguous_dma(reason="small gains and sinks"):
                for dst, src in loads:
                    sp.dma_start(dst, src).then_inc(c_ld, 16)
            with sp.Fori(0, (STEPS - 3) // 2) as i:
                for c in (2, 3):
                    s = Step(c, i)
                    sp.wait_ge(h_xn, s.v - 1)
                    load_x(-1, s, xp, xsm)
            sp.wait_ge(h_xn, STEPS - 2)
            load_x(-1, Step(STEPS - 1), xp, xsm)
            sp.dma_start(ys, xp).then_inc(xy_cp, 16)
            sp.dma_start(ysm, xsm).then_inc(xy_cp, 16)
            for o, i in ((nk_s, cache_k), (nv_s, cache_v)):
                for l in range(DEPTH):
                    sp.dma_start(o[l, :, 0:WINDOW - DEC_SEQ].rearrange("b w g d -> b (w g d)"),
                                 i[l, :, DEC_SEQ:WINDOW].rearrange("b w g d -> b (w g d)")).then_inc(kc_out, 16)

            E = Step(STEPS - 1)
            with sp.Fori(0, DEPTH) as L:
                def at(x):
                    return x[bass.ds(L, 1)]
                sp.wait_ge(h_lo, (L + 1) * STEPS)
                for dst, src in ((ck, cache_k), (cv, cache_v)):
                    sp.dma_start(dst, at(src).rearrange("o b w g d -> w (o b) (g d)")).then_inc(ckv_ld, 16)
                sp.wait_ge(a_qk, L * STEPS + 1)
                for o, c0 in ((nk_s, A_W), (nv_s, A_W + KV_W)):
                    for q in range(DEC_BATCH):
                        sp.dma_start(o[bass.ds(L, 1), q, WINDOW - DEC_SEQ:WINDOW].rearrange("o w g d -> (o w) (g d)"),
                                     land[q * DEC_SEQ:(q + 1) * DEC_SEQ, 0, c0:c0 + KV_W]).then_inc(kvs_out, 16)
                store_mix("A", L, Step(0))
                load_states("B0", L)
                store_mix("A", L, Step(1))
                store_mix("A", L, Step(2))
                with sp.Fori(0, (STEPS - 3) // 2) as i:
                    for c in (3, 4):
                        store_mix("A", L, Step(c, i))
                for o, c0 in ((nk_p, A_W), (nv_p, A_W + KV_W)):
                    sp.dma_start(at(o).rearrange("o n w g d -> (o n w) (g d)"),
                                 land[:, E.par, c0:c0 + KV_W]).then_inc(kv_out, 16)
                for ph in ("B0", "B1"):
                    for h in range(2):
                        sp.wait_ge(b_su, bn(ph, L, Step(0)) + 1)
                        dst = at(nst_s)[:, :, 2 * hb(ph) + h, :, :].rearrange("o b k v -> k (o b) v")
                        sp.dma_start(dst, stS[:, h, :, :]).then_inc(sts_out, 16)
                    if ph == "B0":
                        sp.wait_ge(sts_out, (L * 2 + 1) * 32)
                        load_states("B1", L)
                    for c in range(3):
                        store_mix(ph, L, Step(c))
                    with sp.Fori(0, (STEPS - 5) // 2) as i:
                        for c in (3, 4):
                            store_mix(ph, L, Step(c, i))
                    store_mix(ph, L, E - 1)
                    if ph == "B1":
                        sp.wait_ge(xy_cp, 32)
                        sp.wait_ge(b_qk, (L + 1) * 2 * STEPS)
                        for c in range(2):
                            load_x(L, Step(c), ys, ysm)
                        sp.wait_ge(sts_out, (L * 2 + 2) * 32)
                        for c in range(2):
                            load_mixed(L, Step(c))
                    store_mix(ph, L, E)
                    sp.wait_ge(b_su, bn(ph, L, E) + 1)
                    for h in range(2):
                        sp.dma_start(at(nst_p)[:, 0, 2 * hb(ph) + h, :, :].rearrange("o k v -> (o k) v"),
                                     state[hb(ph)][:, h * P:(h + 1) * P]).then_inc(st_out, 16)

                def o_step(s, loads=True):
                    if loads:
                        sp.wait_ge(o_ms, L * STEPS + s.v + 1)
                        load_mixed(L, s + 2)
                    sp.wait_ge(dve_piece, piece("O", L, s, 1) + 2)
                    sp.dma_start(xs(s, ys, ysm), xt_[0:s.rows, s.par, :]).then_inc(y_out[s.par], 16)
                    if loads:
                        alone(sp, y_out[s.par], 16 * (L * (9 - s.par) + s.half + 1))
                        sp.wait_ge(h_xn, hn(L, s) + 1)
                        load_x(L, s + 2, ys, ysm)

                o_step(Step(0))
                with sp.Fori(0, (STEPS - 3) // 2) as i:
                    for c in (1, 2):
                        o_step(Step(c, i))
                o_step(E - 1, False)
                o_step(E, False)
                alone(sp, y_out[0], 16 * (L + 1) * 9)
                alone(sp, y_out[1], 16 * (L + 1) * 8)
            sp.wait_ge(kc_out, 2 * DEPTH * 16)
            sp.wait_ge(kvs_out, DEPTH * 256)
            sp.wait_ge(st_out, 64 + DEPTH * 64)
            sp.wait_ge(sts_out, DEPTH * 64)
            sp.wait_ge(kv_out, DEPTH * 32)
            for p in range(2):
                sp.wait_ge(y_out[p], 16 * DEPTH * (9 - p))
                sp.wait_ge(mix_out[p], 16 + 16 * DEPTH * MIX_OUT[p])


CONST_LOADS = 10 + DEPTH * 12
_INS = ["x_prompt", "x_sample", "cache_swa_k", "cache_swa_v", "state_ret", "w_in", "w_out", "norm_g",
        "q_norm_g", "k_norm_g", "sinks"]
_CONSTS = ["rope_ap", "rope_as", "rope_bp", "rope_bs", "mask_a", "mask_s", "decay", "decay_s", "cols", "ident"]
_OUTS = [(1, SEQ, D_MODEL), (DEC_BATCH, DEC_SEQ, D_MODEL),
         (DEPTH, 1, WINDOW, A_KV, A_DIM), (DEPTH, 1, WINDOW, A_KV, A_DIM), (DEPTH, 1, B_HEADS, DK, DV),
         (DEPTH, DEC_BATCH, WINDOW, A_KV, A_DIM), (DEPTH, DEC_BATCH, WINDOW, A_KV, A_DIM),
         (DEPTH, DEC_BATCH, B_HEADS, DK, DV)]


def kernel(**inputs):
    import numpy as _np
    import concourse.bacc as _bacc
    from concourse import mybir as _mybir
    from concourse.bass_utils import run_bass_kernel_spmd as _run

    nc = _bacc.Bacc("TRN2", target_bir_lowering=False, num_devices=1)
    arrays, args = {}, []
    tables = constants()
    for name in _INS + _CONSTS:
        a = _np.ascontiguousarray(inputs[name] if name in _INS else tables[name])
        arrays[f"in_{name}"] = a
        args.append(nc.dram_tensor(f"in_{name}", a.shape, _mybir.dt.from_np(a.dtype), kind="ExternalInput").ap())
    for i, shape in enumerate(_OUTS):
        args.append(nc.dram_tensor(f"out_{i}", shape, _mybir.dt.float32, kind="ExternalOutput").ap())
    args.append(nc.dram_tensor("mixed", (ROWS, MIX_W), _mybir.dt.float32).ap())
    trunk(nc, *args)
    r = _run(nc, [arrays], core_ids=[0])
    return tuple(r.results[0][f"out_{i}"] for i in range(len(_OUTS)))
```

```python
import concourse.bass as bass
from concourse import mybir
from contextlib import ExitStack

F32 = mybir.dt.float32
F16 = mybir.dt.float16
BF16 = mybir.dt.bfloat16
I32 = mybir.dt.int32
U16 = mybir.dt.uint16
ALU = mybir.AluOpType
ACT = mybir.ActivationFunctionType
AX = mybir.AxisListType

D_MODEL, SEQ, DEPTH, DEC_BATCH, DEC_SEQ, PAST = 1024, 2048, 2, 8, 4, 2048
A_HEADS, A_KV, A_DIM, WINDOW = 8, 2, 64, 128
A_GROUP = A_HEADS // A_KV
ROT = A_DIM // 4
B_HEADS, DK, DV = 4, 128, 128
EPS = 1e-6
P = 128
KT = D_MODEL // P
TILES = SEQ // P
STEPS = TILES + 1
NS = DEC_BATCH * DEC_SEQ
ROWS = SEQ + NS
A_W, KV_W, B_W = A_HEADS * A_DIM, A_KV * A_DIM, B_HEADS * DK
IN_W = 2 * A_W + 2 * KV_W + 4 * B_W
MIX_W = A_W + B_W
N_A = 2 * A_W + 2 * KV_W
N_B = 4 * 2 * DK
N_O = D_MODEL
DVE_KT = 3
H_SCALE = 2.0 ** 10
TOP = 2.0 ** -14
TINY = 1e-30
NEG = -3e38
QK_TOP = 2.0 ** 11
P_TOP = 2.0 ** 14
V_DOWN = 2.0 ** -19
GAIN_MIN = 2.0 ** -40
MAGIC = 1597463007.0
NEWTON = 3
RSQRT_LINKS = 2 + 3 * NEWTON
CH_A = ((0, A_W), (A_W, 2 * KV_W), (A_W + 2 * KV_W, A_W))
CH_2 = ((0, 512), (512, 512))
PIECE0 = {"A": 0, "B0": 3 * STEPS, "B1": 5 * STEPS, "O": 7 * STEPS}
PIECES = 9 * STEPS
APIECE0 = {"A": 0, "B0": 3 * STEPS, "B1": 4 * STEPS}
APIECES = 5 * STEPS
MIX_OUT = (26, 25)
MIX_OUT0 = {"A": (0, 0), "B0": (9, 8), "B1": (17, 17)}
KEYS = DEC_BATCH * WINDOW


def lam(h):
    return 1.0 - 2.0 ** (-5.0 - h)


def bfloat16_bits(x):
    import numpy as np
    return (np.ascontiguousarray(x, dtype=np.float32).view(np.uint32) >> 16).astype(np.uint16)


def constants():
    import numpy as np
    f = np.float32
    c = {}
    pos = np.arange(SEQ)
    ps = PAST + np.arange(NS) % DEC_SEQ
    for name, theta, half in (("a", 500000.0, ROT // 2), ("b", 10000.0, DK // 2)):
        inv = (f(theta) ** (-np.arange(half, dtype=f) / f(half))).astype(f)
        for tag, p in (("p", pos), ("s", ps)):
            ang = (p.astype(f)[:, None] * inv[None, :]).astype(f).astype(np.float64)
            t = np.stack([np.cos(ang), np.sin(ang)], 1).astype(f)
            if tag == "p":
                t = t.reshape(TILES, P, 2, half).transpose(1, 0, 2, 3)
            c[f"rope_{name}{tag}"] = np.ascontiguousarray(t)
    i = np.arange(P)[:, None]
    j = np.arange(P)[None, :]
    cur = np.where(j <= i, 0.0, NEG)
    prev = np.where(j > i, 0.0, NEG)
    none = np.full((P, P), NEG)
    m = np.stack([np.concatenate(x, 1) for x in ((cur, prev), (prev, cur), (none, cur))], 1)
    c["mask_a"] = bfloat16_bits(m)
    tok = np.arange(P) % NS
    b, ti = tok // DEC_SEQ, tok % DEC_SEQ
    kb = np.concatenate([np.arange(KEYS) // WINDOW, np.arange(NS) // DEC_SEQ])
    kj = np.concatenate([np.arange(KEYS) % WINDOW, WINDOW + np.arange(NS) % DEC_SEQ])
    diff = ti[:, None] + WINDOW - kj[None, :]
    ok = (b[:, None] == kb[None, :]) & (diff >= 0) & (diff < WINDOW)
    c["mask_s"] = bfloat16_bits(np.where(ok, 0.0, NEG))
    dec = np.zeros((P, B_HEADS, P))
    decs = np.zeros((NS, B_HEADS, NS))
    cols = np.zeros((P, 32))
    r = np.arange(P)
    rs = np.arange(NS) % DEC_SEQ
    bs = np.arange(NS) // DEC_SEQ
    for h in range(B_HEADS):
        dec[:, h, :] = np.where(j >= i, lam(h) ** -(i + 1.0), 0.0) * DK ** -0.5
        ok = (bs[:, None] == bs[None, :]) & (rs[None, :] >= rs[:, None])
        decs[:, h, :] = np.where(ok, lam(h) ** -(rs[:, None] + 1.0), 0.0) * DK ** -0.5
        q, k = lam(h) ** (r + 1.0), lam(h) ** (P - 1.0 - r) * DK ** -0.5
        qs, ks = lam(h) ** (rs + 1.0), lam(h) ** (DEC_SEQ - 1.0 - rs) * DK ** -0.5
        cols[:, h], cols[:, 4 + h], cols[:, 8 + h] = q * q / DV, q, k
        cols[:NS, 12 + h], cols[:NS, 16 + h], cols[:NS, 20 + h] = qs * qs / DV, qs, ks
    cols[:NS, 24:32] = bs[:, None] == np.arange(DEC_BATCH)[None, :]
    c["decay"], c["decay_s"], c["cols"] = dec.astype(f), decs.astype(f), cols.astype(f)
    c["ident"] = np.eye(P, dtype=f)
    return c


class Step:

    def __init__(self, c, i=0):
        self.v, self.half, self.par = c + 2 * i, c // 2 + i, c % 2
        self.fixed = isinstance(i, int)
        self.sample = self.fixed and c == 0
        self.first = self.fixed and c == 1
        self.rows = NS if self.sample else P
        self.tile = self.v - 1
        self.col = SEQ if self.sample else self.tile * P
        self.c, self.i = c, i

    def __add__(self, d):
        return Step(self.c + d, self.i)

    def __sub__(self, d):
        return Step(self.c - d, self.i)


class Chain:

    def __init__(self, eng, sem, links, times):
        self.eng, self.sem, self.links, self.base, self.n = eng, sem, links, times * links, 0

    def __call__(self, ins):
        self.n += 1
        ins.then_inc(self.sem, 1)
        self.eng.wait_ge(self.sem, self.base + self.n)

    def end(self, unwaited=0):
        assert self.n + unwaited == self.links, (self.n, self.links)


def early(c, i=0):
    s = Step(c, 2 * i)
    s.ring, s.turn = c % 4, c // 4 + i
    return s


def trunk(nc, x_prompt, x_sample, cache_k, cache_v, state_ret, w_in, w_out, norm_g, q_g, k_g, sinks,
          rope_ap, rope_as, rope_bp, rope_bs, mask_a, mask_s, decay, decay_s, cols, ident,
          y_p, y_s, nk_p, nv_p, nst_p, nk_s, nv_s, nst_s, mixed):
    with ExitStack() as ctx:
        def sb(name, shape, dt=F32):
            return ctx.enter_context(nc.sbuf_tensor(name, shape, dt))

        def sem(name):
            return ctx.enter_context(nc.semaphore(name))

        hT = sb("hT", [P, 2, KT, ROWS], F16)
        w_a = sb("w_a", [P, KT * N_A])
        w_b = sb("w_b", [P, KT * N_B])
        w_tmp = sb("w_tmp", [P, 512])
        land = sb("land", [P, 2, 2 * A_W + 2 * KV_W])
        mix = sb("mix", [P, 2, A_W])
        r1 = sb("r1", [P, 4096])
        r2 = sb("r2", [P, 4384])
        t_rap, t_ras = sb("t_rap", [P, TILES, 2, ROT // 2]), sb("t_ras", [NS, 2, ROT // 2])
        t_rbp, t_rbs = sb("t_rbp", [P, TILES, 2, DK // 2]), sb("t_rbs", [NS, 2, DK // 2])
        t_ma, t_ms = sb("t_ma", [P, 3, 2 * P], U16), sb("t_ms", [P, KEYS + NS], U16)
        t_dec, t_decs = sb("t_dec", [P, B_HEADS, P]), sb("t_decs", [NS, B_HEADS, NS])
        t_cols, eye = sb("t_cols", [P, 32]), sb("eye", [P, P])
        g_all = sb("g_all", [P, DEPTH, KT])
        qk_all = sb("qk_all", [P, DEPTH, 2, A_DIM])
        sk_all = sb("sk_all", [P, DEPTH, A_HEADS])
        sks_all = sb("sks_all", [P, DEPTH, A_KV])
        qk_g, sk, sks = sb("qk_g", [P, 2, A_DIM]), sb("sk", [P, A_HEADS]), sb("sks", [P, A_KV])
        nsk, nsks = sb("nsk", [P, A_HEADS]), sb("nsks", [P, A_KV])
        kT_hi, kT_lo = sb("kT_hi", [P, A_KV, 2, P], F16), sb("kT_lo", [A_DIM, A_KV, 2, P], F16)
        g_mx, qk_s, unqk = sb("g_mx", [P, 2]), sb("qk_s", [P, 2]), sb("unqk", [P, 2])
        eye16 = sb("eye16", [P, P], F16)
        ones = sb("ones", [P, KT])
        g_cur = sb("g_cur", [P, KT])
        w_mx, w_m1, w_am, w_q, w_s, w_gs = (sb(n, [P, m]) for n, m in (
            ("w_mx", KT), ("w_m1", 1), ("w_am", 1), ("w_q", 1), ("w_s", 1), ("w_gs", KT)))
        cs = {k: sb(f"cs_{k}", [P, 8]) for k in ("A", "B0", "B1", "O")}
        ss, rs, rt = sb("ss", [P, 10]), sb("rs", [P, 2, 10]), sb("rt", [P, 10])
        mr, nm, sd, es, rsum, rr = (sb(n, [P, 2, A_GROUP]) for n in ("mr", "nm", "sd", "es", "rsum", "rr"))
        oss, oms, oy, ot = (sb(n, [P, 2]) for n in ("oss", "oms", "oy", "ot"))
        mq, mqq, minv, mdd = sb("mq", [P, 1]), sb("mqq", [P, 2]), sb("minv", [P, 2]), sb("mdd", [P, 2])
        xss, xms, xy, xt = (sb(n, [P, m]) for n, m in (("xss", 2), ("xms", 2), ("xy", 4), ("xt", 2)))

        ck = r1[:, 0:1024].rearrange("p (b c) -> p b c", c=KV_W)
        cv = r1[:, 1024:2048].rearrange("p (b c) -> p b c", c=KV_W)
        kts = r1[:, 2048:3072]
        knew = r1[:, 3072:3072 + 2 * NS].rearrange("p (g n) -> p g n", g=2)
        stS = r1[:, 0:2048].rearrange("p (h b v) -> p h b v", h=2, b=DEC_BATCH)
        qtm = r1[:, 2048:2048 + 2 * 288].rearrange("p (h n) -> p h n", h=2)
        t1 = r1[:, 3072:3584]
        t2 = r1[:, 3584:4096]
        mxt = r1[:, 0:2048].rearrange("p (b n) -> p b n", b=2)
        xt_ = r1[:, 2048:4096].rearrange("p (b n) -> p b n", b=2)
        sq = r2[:, 0:640]
        rp1, rp2 = (r2[:, o:o + 160].rearrange("p (h c d) -> p h c d", c=2, d=ROT // 2) for o in (0, 160))
        k16 = r2[:, 640:832].bitcast(F16)
        qT = r2[:, 896:1408]
        qT16 = qT.bitcast(F16)
        q16 = r2[:, 1664:2176].bitcast(F16).rearrange("p (h e d) -> p h e d", e=2, d=A_DIM)
        v16 = r2[:, 1408:1664].bitcast(F16).rearrange("p (b e n) -> p b e n", b=2, e=2)
        vd = r2[:, 1664:2176].rearrange("p (b n) -> p b n", b=2)
        prob = r2[:, 2176:3232]
        pT = r2[:, 3232:4384]
        pT16 = r2[:, 3232:4256].bitcast(F16).rearrange("p (e n) -> p e n", e=2)
        qkT = r2[:, 0:512]
        osq = r2[:, 640:896]
        state = (r2[:, 896:1152], r2[:, 1408:1664])
        stm = r2[:, 1152:1408]
        vbd = r2[:, 2176:2176 + 2048].rearrange("p (h b v) -> p h b v", h=2, b=DEC_BATCH)
        xn = r2[:, 288:1312]
        x4 = r1[:, 0:4096].rearrange("p (q n) -> p q n", q=4)
        xn2 = r2[:, 3360:4384]
        w_tmp2 = r2[:, 1312:1824]
        xsq = r2[:, 1824:2848]
        mT = tuple(r2[:, o:o + 1024].bitcast(F16).rearrange("p (k e t) -> p k e t", k=KT, e=2)
                   for o in (2336, 1312))
        msc = r2[:, 3360:4384]

        PA, PB, TK, S0, S1, X0, X1, OB = (
            ctx.enter_context(nc.psum_tensor(n, [P, 512], F32))
            for n in ("PA", "PB", "TK", "S0", "S1", "X0", "X1", "OB"))
        PP, SS, XX = (PA, PB), (S0, S1), (X0, X1)

        id_ld, c_ld, xy_cp = sem("identity_gains_loaded"), sem("tables_loaded"), sem("x_copied")
        x4_ld = tuple(sem(f"prologue_x_loaded{q}") for q in range(4))
        init = sem("memsets_done")
        pe_piece, act_piece, dve_piece = sem("pe_piece"), sem("act_piece"), sem("dve_piece")
        w_ld = (sem("w_loaded_lo"), sem("w_loaded_hi"))
        w_max, w_all, w_sc, w_rd = sem("w_max"), sem("w_allreduced"), sem("w_scales"), sem("w_ready")
        a_qk, a_tk, a_te = sem("a_qk_ready"), sem("a_transposed"), sem("a_transposes_out")
        s_ct, s_ce = sem("cached_keys_transposed"), sem("cached_keys_out")
        qk_hi, qk_lo = sem("qk_hi"), sem("qk_lo")
        a_s, a_sm, a_ex = sem("a_scores"), sem("a_masked"), sem("a_probs")
        a_pt, a_po, a_pv, a_mx = sem("a_probsT"), sem("a_probsT_out"), sem("a_pv"), sem("a_mixed")
        a_pl = sem("a_probsT_lo")
        b_qk, b_tk, b_te = sem("b_qk_ready"), sem("b_transposed"), sem("b_transposes_out")
        b_st, b_dm, b_o = sem("b_scoresT"), sem("b_decayed"), sem("b_out")
        b_su, b_sq, b_mx, b_vb = sem("b_state"), sem("b_squares"), sem("b_mixed"), sem("b_vbd")
        mix_out = (sem("mix_out0"), sem("mix_out1"))
        kv_out, st_out, sts_out = sem("kv_out"), sem("state_out"), sem("sample_state_out")
        kvs_out, kc_out = sem("kv_sample_out"), sem("cache_shift_out")
        ckv_ld, sts_ld = sem("cache_loaded"), sem("sample_state_loaded")
        mx_ld, x_ld = (sem("mixed_loaded0"), sem("mixed_loaded1")), (sem("x_loaded0"), sem("x_loaded1"))
        y_out = (sem("y_out0"), sem("y_out1"))
        o_sc, o_ms, o_tm, o_hi, o_lo = (sem(n) for n in (
            "o_scale", "o_scaled", "o_transposed", "o_hi", "o_lo"))
        h_sq, h_rs, h_xn, h_t, h_hi, h_lo = (sem(n) for n in (
            "h_squares", "h_rstd", "h_normed", "h_transposed", "h_hi", "h_lo"))
        alone_count = sem("alone_count")
        ch_wm, ch_ws, ch_wp = sem("chain_w_max"), sem("chain_w_scale"), sem("chain_w_pool")
        ch_an, ch_asm, ch_amx = sem("chain_a_norm"), sem("chain_a_softmax"), sem("chain_a_mix")
        ch_ams, ch_bo, ch_om = sem("chain_a_mix_sample"), sem("chain_b_out"), sem("chain_o_scale")
        ch_ou, ch_p, ch_h = sem("chain_o_unscale"), sem("chain_prologue"), sem("chain_h")
        ch_l, ch_wd, ch_asp = sem("chain_layer"), sem("chain_w_vector"), sem("chain_a_softmax_prompt")
        ch_g, ch_v = sem("chain_gains"), sem("chain_v")

        BLOCKS = ("A", "B0", "B1", "O")
        SLOT = {"A": w_a, "B0": w_b, "B1": w_a, "O": w_b}
        WIDTH = {"A": N_A, "B0": N_B, "B1": N_B, "O": N_O}
        CH = {"A": CH_A, "B0": CH_2, "B1": CH_2, "O": CH_2}

        def hb(ph):
            return int(ph[1])

        def an(L, s):
            return L * STEPS + s.v

        def bn(ph, L, s):
            return (L * 2 + hb(ph)) * STEPS + s.v

        def hn(L, s):
            return (L + 1) * STEPS + s.v

        def tn(L, s):
            return L * TILES + s.v - 1

        def pro(L):
            return isinstance(L, int) and L < 0

        def h_banks(L, s):
            return XX if not pro(L) or s.par else (TK, S0)

        def m_banks(s):
            return XX if s.fixed and s.c < 2 else (TK, S0)

        def xn_of(L, s):
            return xn if not pro(L) or s.par else xn2

        def wn(L, kind):
            return L * 4 + BLOCKS.index(kind)

        def lpar(ph, s):
            return (s.par + 1) % 2 if ph == "B0" else s.par

        def mix_count(ph, L, s):
            p = lpar(ph, s)
            return L * MIX_OUT[p] + MIX_OUT0[ph][p] + s.half + 1

        def piece(ph, L, s, p):
            return L * PIECES + PIECE0[ph] + s.v * (3 if ph == "A" else 2) + p

        def bank(ph, s, p):
            if ph == "A":
                return PP[(s.par * 3 + p) % 2]
            return PP[(p + 1) % 2]

        def apiece(ph, L, s, p):
            return L * APIECES + APIECE0[ph] + (s.v * 3 + p if ph == "A" else s.v)

        def w16(kind, k, c, part):
            c0, n = CH[kind][c]
            o = (k * WIDTH[kind] + c0) * 2 + part * n
            return SLOT[kind][:, :].bitcast(F16)[:, o:o + n]

        def raw(kind, k, c=None):
            c0, n = (0, WIDTH[kind]) if c is None else CH[kind][c]
            o = k * WIDTH[kind] + c0
            return SLOT[kind][:, o:o + n]

        def hcols(s):
            return slice(s.col, s.col + s.rows) if s.fixed else bass.ds(s.col, P)

        def alone(eng, semaphore, value):
            eng.wait_ge(semaphore, value)
            eng.sem_inc(alone_count, 1)

        win = w_in.rearrange("l (k p) n -> l p k n", p=P)
        wout = w_out.rearrange("l (k p) n -> l p k n", p=P)

        def load_weights(eng, kind, layer):
            def cols(k, c0, n):
                src = wout if kind == "O" else win
                if isinstance(layer, int):
                    return src[layer, :, k, c0:c0 + n]
                return src[bass.ds(layer, 1), :, k, c0:c0 + n].rearrange("o p n -> (o p) n")

            for k in range(KT):
                s = w_ld[k // 4]
                if kind == "A":
                    for g in range(A_KV):
                        eng.dma_start(raw(kind, k, 0).rearrange("p (h g d) -> p h g d", g=A_KV, d=A_DIM)[:, :, g, :],
                                    cols(k, g * 256, 256).rearrange("p (h d) -> p h d", d=A_DIM)).then_inc(s, 16)
                    eng.dma_start(raw(kind, k)[:, A_W:], cols(k, A_W, N_A - A_W)).then_inc(s, 16)
                elif kind == "O":
                    eng.dma_start(raw(kind, k), cols(k, 0, WIDTH[kind])).then_inc(s, 16)
                else:
                    src = win[:, :, k, N_A:IN_W].rearrange("l p (q n) -> l p q n", q=4)
                    o = hb(kind) * 2 * DK
                    eng.dma_start(raw(kind, k).rearrange("p (q n) -> p q n", q=4),
                                src[bass.ds(layer, 1), :, :, o:o + 2 * DK].rearrange("o p q n -> (o p) q n")
                                ).then_inc(s, 16)

        block = ctx.enter_context(nc.Block())

        @block.tensor
        def _(pe):
            def proj(ph, L, s, p, k0, k1):
                out = bank(ph, s, p)
                n = CH[ph][p][1]
                j = piece(ph, L, s, p)
                if k0 == 0:
                    pe.wait_ge(dve_piece, j + 1 if ph == "A" and s.sample and p == 0 else j)
                    if ph == "O" and p == 0:
                        pe.wait_ge(o_lo, L * STEPS + s.v + 1)
                for k in range(k0, k1):
                    for part, wpart in ((0, 0), (0, 1), (1, 0)):
                        if ph == "O":
                            lhs = mT[s.par][:, k, part, 0:s.rows]
                        else:
                            lhs = hT[:, part, k, hcols(s)]
                        last = nc.tensor.matmul(
                            out[0:s.rows, 0:n], lhs, w16(ph, k, p, wpart),
                            start=(k == 0 and part == 0 and wpart == 0),
                            stop=(k == KT - 1 and part == 1))
                if k1 == KT:
                    last.then_inc(pe_piece, 1)

            def a_T(L, s):
                if s.sample:
                    pe.wait_ge(a_qk, an(L, s) + 1)
                    alone(pe, ckv_ld, (L + 1) * 32)
                    for g in range(A_KV):
                        for h in range(A_GROUP):
                            q, o = g * A_GROUP + h, (h * A_KV + g) * A_DIM
                            nc.tensor.transpose(TK[0:A_DIM, q * NS:(q + 1) * NS],
                                                land[0:NS, 0, o:o + A_DIM], eye[0:NS, 0:NS])
                        o = A_W + g * A_DIM
                        nc.tensor.transpose(TK[0:A_DIM, (A_HEADS + g) * NS:(A_HEADS + g + 1) * NS],
                                            land[0:NS, 0, o:o + A_DIM], eye[0:NS, 0:NS])
                    last = cached_keys(0)
                else:
                    if s.first:
                        pe.wait_ge(a_po, 2 * an(L, s))
                    pe.wait_ge(qk_lo, tn(L, s) + 1)
                    for i in range(A_HEADS):
                        nc.tensor.transpose(TK[:, :].bitcast(F16)[:, i * P:(i + 1) * P],
                                            q16[:, i, :, :].rearrange("p e d -> p (e d)"), eye16[:, :])
                    if not s.first:
                        pe.wait_ge(a_sm, 2 * an(L, s))
                    S16 = S0[:, :].bitcast(F16)
                    for g in range(A_KV):
                        nc.tensor.transpose(S16[:, g * P:(g + 1) * P], k16[:, g * P:(g + 1) * P], eye16[:, :])
                    for g in range(A_KV):
                        o = A_KV * P + g * A_DIM
                        last = nc.tensor.transpose(S16[0:A_DIM, (2 + g) * P:(3 + g) * P],
                                                   k16[:, o:o + A_DIM], eye16[:, :])
                last.then_inc(a_tk, 1)

            def cached_keys(g):
                for q in range(DEC_BATCH):
                    last = nc.tensor.transpose(XX[q // 4][0:A_DIM, (q % 4) * P:(q % 4 + 1) * P],
                                               ck[:, q, g * A_DIM:(g + 1) * A_DIM], eye[:, :])
                return last

            def a_S(L, s, g):
                n = an(L, s)
                pe.wait_ge(a_te, n + 1)
                if not (s.sample and g == 0):
                    pe.wait_ge(a_sm, 2 * n + g)
                if s.sample:
                    if g == 1:
                        pe.wait_ge(a_po, 2 * n + 1)
                    lhs = qT[0:A_DIM, g * P:(g + 1) * P]
                    for q in range(2):
                        nc.tensor.matmul(SS[q][:, :], lhs, kts[0:A_DIM, q * 512:(q + 1) * 512],
                                         start=True, stop=True)
                    last = nc.tensor.matmul(TK[:, 0:NS], lhs, knew[0:A_DIM, g, :], start=True, stop=True)
                else:
                    for h in range(A_GROUP):
                        out = SS[h // 2][:, (h % 2) * 256:(h % 2) * 256 + 256]
                        q = (h * A_KV + g) * P
                        nc.tensor.matmul(out, qT16[:, q:q + P], kT_hi[:, g, :, :].rearrange("p b t -> p (b t)"),
                                         start=True, stop=False)
                        last = nc.tensor.matmul(out, qT16[0:A_DIM, q:q + P],
                                                kT_lo[:, g, :, :].rearrange("p b t -> p (b t)"),
                                                start=False, stop=True)
                last.then_inc(a_s, 1)

            def a_PT(L, s, g):
                if s.sample and g == 0:
                    pe.wait_ge(s_ce, L + 1)
                pe.wait_ge(a_ex, 2 * an(L, s) + g + 1)
                for q in range(8):
                    last = nc.tensor.transpose(XX[q // 4][:, (q % 4) * P:(q % 4 + 1) * P],
                                               prob[:, q * P:(q + 1) * P], eye[:, :])
                if s.sample:
                    last = nc.tensor.transpose(TK[0:NS, P:2 * P], prob[:, KEYS:KEYS + NS], eye[:, :])
                last.then_inc(a_pt, 1)

            def a_PV(L, s, g):
                n = an(L, s)
                if s.sample:
                    pe.wait_ge(a_po, 2 * n + g + 1)
                else:
                    pe.wait_ge(a_pl, 2 * tn(L, s) + g + 1)
                if not (s.sample and g == 0):
                    pe.wait_ge(a_mx, 2 * n + g)
                if s.sample:
                    for q in range(DEC_BATCH):
                        nc.tensor.matmul(OB[:, 0:A_DIM], pT[:, q * P:(q + 1) * P],
                                         cv[:, q, g * A_DIM:(g + 1) * A_DIM], start=(q == 0), stop=False)
                    o = A_W + KV_W + g * A_DIM
                    last = nc.tensor.matmul(OB[:, 0:A_DIM], pT[0:NS, KEYS:KEYS + P],
                                            land[0:NS, 0, o:o + A_DIM], start=False, stop=True)
                else:
                    for h in range(A_GROUP):
                        for q in range(2):
                            o = (h * 2 + q) * P
                            for e, ve in ((0, 0), (0, 1), (1, 0)):
                                last = nc.tensor.matmul(OB[:, h * A_DIM:(h + 1) * A_DIM], pT16[:, e, o:o + P],
                                                        v16[:, q, ve, g * A_DIM:(g + 1) * A_DIM],
                                                        start=(q == 0 and e == ve), stop=(q == 1 and e == 1))
                last.then_inc(a_pv, 1)

            def b_T(ph, L, s):
                b, r = lpar(ph, s), s.rows
                alone(pe, b_qk, bn(ph, L, s) + 1)
                for i in range(4):
                    last = nc.tensor.transpose(TK[:, i * r:(i + 1) * r], land[0:r, b, i * P:(i + 1) * P],
                                               eye[0:r, 0:r])
                last.then_inc(b_tk, 1)

            def b_ST(ph, L, s):
                r = s.rows
                if s.first:
                    pe.wait_ge(b_su, bn(ph, L, s))
                pe.wait_ge(b_te, bn(ph, L, s) + 1)
                for h in range(2):
                    last = nc.tensor.matmul(S0[0:r, h * r:(h + 1) * r], qkT[:, (2 + h) * r:(3 + h) * r],
                                            qkT[:, h * r:(h + 1) * r], start=True, stop=True)
                last.then_inc(b_st, 1)

            def b_OS(ph, L, s):
                n, b, r, st = bn(ph, L, s), lpar(ph, s), s.rows, state[hb(ph)]
                pe.wait_ge(b_dm, n + 1)
                pe.wait_ge(act_piece, apiece(ph, L, s, 1) + 1)
                if not s.sample:
                    pe.wait_ge(b_su, n)
                    pe.wait_ge(b_mx, n)
                else:
                    pe.wait_ge(sts_ld, (L * 2 + hb(ph) + 1) * 32)
                    if hb(ph) == 1:
                        pe.wait_ge(b_mx, n)
                    alone(pe, b_vb, L * 2 + hb(ph) + 1)
                for h in range(2):
                    v = land[0:r, b, 512 + h * P:512 + (h + 1) * P]
                    nc.tensor.matmul(OB[0:r, h * P:(h + 1) * P], stm[0:r, h * r:(h + 1) * r], v,
                                     start=True, stop=False)
                    if s.sample:
                        for q in range(DEC_BATCH):
                            last = nc.tensor.matmul(OB[0:r, h * P:(h + 1) * P], qtm[:, h, q * NS:(q + 1) * NS],
                                                    stS[:, h, q, :], start=False, stop=(q == DEC_BATCH - 1))
                    else:
                        last = nc.tensor.matmul(OB[0:r, h * P:(h + 1) * P], qkT[:, h * P:(h + 1) * P],
                                                st[:, h * P:(h + 1) * P], start=False, stop=True)
                for h in range(2):
                    k = land[0:r, b, (2 + h) * P:(3 + h) * P]
                    if s.sample:
                        for q, bk in enumerate(((S1, X0), (X1, S0))[h]):
                            last = nc.tensor.matmul(bk[:, :], k, vbd[0:r, h, 4 * q:4 * q + 4, :],
                                                    start=True, stop=True)
                    else:
                        last = nc.tensor.matmul(S1[:, h * P:(h + 1) * P], k, vd[:, b, h * P:(h + 1) * P],
                                                start=True, stop=True)
                last.then_inc(b_o, 1)

            def tr8(src, banks, r):
                for k in range(KT):
                    last = nc.tensor.transpose(banks[k // 4][:, (k % 4) * P:(k % 4) * P + r],
                                               src[0:r, k * P:(k + 1) * P], eye[0:r, 0:r])
                return last

            def o_Tm(L, s):
                alone(pe, o_ms, L * STEPS + s.v + 1)
                tr8(msc, m_banks(s), s.rows).then_inc(o_tm, 1)

            def h_T(L, s):
                n = hn(L, s)
                if not pro(L):
                    pe.wait_ge(h_lo, n)
                elif not (s.fixed and s.c < 2):
                    pe.wait_ge(h_lo, s.v - 1)
                alone(pe, h_xn, n + 1)
                tr8(xn_of(L, s), h_banks(L, s), s.rows).then_inc(h_t, 1)

            def step2(ph, L, s, f):
                for p in range(2):
                    for half in range(2):
                        proj(ph, L, s, p, half * KT // 2, (half + 1) * KT // 2)
                        for work in f[2 * p + half]:
                            work()

            def a_step(L, s, f):
                q = KT // 4
                proj("A", L, s, 0, 0, 3 * q)
                f[0]()
                proj("A", L, s, 0, 3 * q, KT)
                f[1]()
                proj("A", L, s, 1, 0, KT)
                f[2]()
                proj("A", L, s, 2, 0, 3 * q)
                f[3]()
                proj("A", L, s, 2, 3 * q, KT)

            def a_work(L, s, old=True):
                late = old and not (s - 2).sample

                def f0():
                    if old:
                        a_PV(L, s - 2, 0)
                    if old and not late:
                        a_PT(L, s - 2, 1)
                    a_T(L, s - 1)
                    if late:
                        a_PT(L, s - 2, 1)

                def f1():
                    a_S(L, s - 1, 0)

                def f2():
                    if old:
                        a_PV(L, s - 2, 1)
                    if (s - 1).sample:
                        cached_keys(1).then_inc(s_ct, 1)

                def f3():
                    a_PT(L, s - 1, 0)
                    a_S(L, s - 1, 1)

                return [f0, f1, f2, f3]

            def b_work(ph, L, s):
                return [[lambda: b_T(ph, L, s - 1)], [lambda: b_ST(ph, L, s - 1)],
                        [lambda: b_OS(ph, L, s - 1)], []]

            pe.wait_ge(id_ld, ID_LOADS * 16)
            for c in range(2):
                h_T(-1, Step(c))
            with pe.Fori(0, (STEPS - 3) // 2) as i:
                h_T(-1, Step(2, i))
                h_T(-1, Step(3, i))
            h_T(-1, Step(STEPS - 1))

            def layer(L, last):
                E = Step(STEPS - 1)
                pe.wait_ge(h_lo, (L + 1) * STEPS)
                pe.wait_ge(w_rd, wn(L, "A") + 1)
                nop = [lambda: None] * 4
                a_step(L, Step(0), nop)
                a_step(L, Step(1), a_work(L, Step(1), False))
                a_step(L, Step(2), a_work(L, Step(2)))
                with pe.Fori(0, (STEPS - 3) // 2) as i:
                    for c in (3, 4):
                        a_step(L, Step(c, i), a_work(L, Step(c, i)))

                pe.wait_ge(w_rd, wn(L, "B0") + 1)
                step2("B0", L, Step(0), [
                    [lambda: a_PV(L, E - 1, 0), lambda: a_T(L, E), lambda: a_PT(L, E - 1, 1)],
                    [lambda: a_PV(L, E - 1, 1), lambda: a_S(L, E, 0)],
                    [],
                    [lambda: a_PT(L, E, 0), lambda: a_S(L, E, 1)]])
                step2("B0", L, Step(1), [
                    [lambda: a_PV(L, E, 0), lambda: b_T("B0", L, Step(0))],
                    [lambda: a_PT(L, E, 1), lambda: b_ST("B0", L, Step(0))],
                    [lambda: a_PV(L, E, 1)],
                    [lambda: b_OS("B0", L, Step(0))]])
                for ph, lo in (("B0", 2), ("B1", 1)):
                    if ph == "B1":
                        pe.wait_ge(w_rd, wn(L, "B1") + 1)
                        step2("B1", L, Step(0), b_work("B0", L, E + 1))
                    for c in range(lo, 3):
                        step2(ph, L, Step(c), b_work(ph, L, Step(c)))
                    with pe.Fori(0, (STEPS - 3) // 2 - hb(ph)) as i:
                        for c in (3, 4):
                            step2(ph, L, Step(c, i), b_work(ph, L, Step(c, i)))
                step2("B1", L, E - 1, b_work("B1", L, E - 1))
                step2("B1", L, E, b_work("B1", L, E)[:3] + [[lambda: b_T("B1", L, E), lambda: o_Tm(L, Step(0))]])

                pe.wait_ge(w_rd, wn(L, "O") + 1)
                step2("O", L, Step(0), [
                    [lambda: b_ST("B1", L, E), lambda: o_Tm(L, Step(1))],
                    [lambda: b_OS("B1", L, E)], [], []])
                def o_work(s):
                    return [[] if s.fixed and s.c == STEPS - 1 else [lambda: o_Tm(L, s + 1)], [],
                            [] if last else [lambda: h_T(L, s - 1)], []]
                for c in (1, 2):
                    step2("O", L, Step(c), o_work(Step(c)))
                with pe.Fori(0, (STEPS - 5) // 2) as i:
                    for c in (3, 4):
                        step2("O", L, Step(c, i), o_work(Step(c, i)))
                step2("O", L, E - 1, o_work(E - 1))
                step2("O", L, E, o_work(E))
                if not last:
                    h_T(L, E)

            with pe.Fori(0, DEPTH - 1) as L:
                layer(L, False)
            layer(DEPTH - 1, True)

        @block.vector
        def _(v):
            V = nc.vector

            def rsqrt(ch, x, y, t):
                ch(V.tensor_scalar(y.bitcast(I32), x.bitcast(I32), 1, None, ALU.logical_shift_right))
                V.tensor_scalar(x, x, -0.5, None, ALU.mult)
                ch(V.tensor_scalar(y.bitcast(I32), y.bitcast(I32), -1.0, MAGIC, ALU.mult, ALU.add))
                for _ in range(NEWTON):
                    ch(V.tensor_tensor(t, y, y, ALU.mult))
                    ch(V.tensor_tensor(t, t, x, ALU.mult))
                    ch(V.scalar_tensor_tensor(out=y, in0=t, scalar=1.5, in1=y, op0=ALU.add, op1=ALU.mult))

            def bc(col, n):
                return col.broadcast_to([col.shape[0], n])

            def w_absmax(L, kind, half):
                v.wait_ge(w_ld[half], 64 * (wn(L, kind) + 3 + 2 * L))
                for k in range(4 * half, 4 * half + 4):
                    last = V.tensor_reduce(w_mx[:, k:k + 1], raw(kind, k), AX.X, ALU.max,
                                           apply_absolute_value=True)
                if half == 1:
                    ch = Chain(v, ch_wm, 2, wn(L, kind))
                    ch(last)
                    ch(V.tensor_tensor(w_mx[:, :], w_mx[:, :], ones[:, :] if kind == "O" else g_cur[:, :],
                                       ALU.mult))
                    V.tensor_reduce(w_m1[:, :], w_mx[:, :], AX.X, ALU.max,
                                    apply_absolute_value=True).then_inc(w_max, 1)
                    ch.end()

            def w_scale(L, kind):
                ch = Chain(v, ch_ws, 4, wn(L, kind))
                v.wait_ge(w_all, wn(L, kind) + 1)
                ch(V.tensor_scalar(w_q[:, :], w_am[:, :], TOP, TINY, ALU.mult, ALU.max))
                ch(V.reciprocal(w_s[:, :], w_q[:, :]))
                V.tensor_scalar(w_gs[:, :], ones[:, :] if kind == "O" else g_cur[:, :], w_s[:, 0:1], None,
                                ALU.mult).then_inc(w_sc, 1)
                c = cs[kind]
                ch(V.tensor_scalar(c[:, 0:1], w_q[:, :], 1.0 if kind == "O" else 1.0 / H_SCALE, None, ALU.mult))
                if kind == "A":
                    V.tensor_scalar(c[:, 2:3], w_s[:, :], H_SCALE * V_DOWN, None, ALU.mult)
                    V.tensor_scalar(c[:, 3:4], c[:, 0:1], c[:, 0:1], 0.5 / (V_DOWN * P_TOP), ALU.mult, ALU.mult)
                if kind[0] == "B":
                    h = 2 * hb(kind)
                    V.tensor_scalar(c[:, 2:4], t_cols[:, 8 + h:10 + h], c[:, 0:1], None, ALU.mult)
                    V.tensor_scalar(c[0:NS, 4:6], t_cols[0:NS, 20 + h:22 + h], c[0:NS, 0:1], None, ALU.mult)
                V.tensor_scalar(c[:, 1:2], c[:, 0:1], 0.5, None, ALU.mult).then_inc(ch_ws, 1)
                ch.end(1)
                alone(v, ch_ws, (wn(L, kind) + 1) * ch.links)

            def w_gain(layer):
                src = g_all[:, layer, :] if isinstance(layer, int) else \
                    g_all[:, bass.ds(layer, 1), :].rearrange("p o k -> p (o k)")
                return V.tensor_copy(g_cur[:, :], src)

            def a_land_q(L, s):
                r, b = s.rows, s.par
                v.wait_ge(act_piece, apiece("A", L, s, 0) + 1)
                q = land[0:r, b, 0:A_W].rearrange("p (h d) -> p h d", d=A_DIM)
                src = bank("A", s, 0)[0:r, 0:A_W].rearrange("p (h d) -> p h d", d=A_DIM)
                g = qk_g[0:r, 0, :].unsqueeze(1).broadcast_to([r, A_HEADS, A_DIM])
                V.scalar_tensor_tensor(out=q, in0=src, scalar=cs["A"][0:r, 0:1], in1=g, op0=ALU.mult,
                                       op1=ALU.mult).then_inc(dve_piece, 1)
                V.tensor_reduce(ss[0:r, 0:8], sq[0:r, 0:A_W].rearrange("p (h d) -> p h d", d=A_DIM),
                                AX.X, ALU.add)

            def a_land_k(L, s):
                r, b = s.rows, s.par
                ch = Chain(v, ch_an, 4 + RSQRT_LINKS, an(L, s))
                v.wait_ge(act_piece, apiece("A", L, s, 1) + 1)
                k = land[0:r, b, A_W:A_W + KV_W].rearrange("p (h d) -> p h d", d=A_DIM)
                src = bank("A", s, 1)[0:r, 0:KV_W].rearrange("p (h d) -> p h d", d=A_DIM)
                g = qk_g[0:r, 1, :].unsqueeze(1).broadcast_to([r, A_KV, A_DIM])
                V.scalar_tensor_tensor(out=k, in0=src, scalar=cs["A"][0:r, 0:1], in1=g, op0=ALU.mult,
                                       op1=ALU.mult).then_inc(dve_piece, 1)
                ch(V.tensor_reduce(ss[0:r, 8:10], sq[0:r, A_W:A_W + KV_W].rearrange("p (h d) -> p h d", d=A_DIM),
                                   AX.X, ALU.add))
                ch(V.tensor_scalar(ss[0:r, :], ss[0:r, :], 1.0 / A_DIM, EPS, ALU.mult, ALU.add))
                y = rs[0:r, b, :]
                rsqrt(ch, ss[0:r, :], y, rt[0:r, :])
                return ch

            def a_rotate(L, s, ch):
                r, b, y = s.rows, s.par, rs[0:s.rows, s.par, :]
                x = land[0:r, b, 0:A_W + KV_W].rearrange("p (h d) -> p h d", d=A_DIM)
                ch(V.tensor_tensor(x, x, y.unsqueeze(2).broadcast_to([r, A_HEADS + A_KV, A_DIM]), ALU.mult))
                tab = t_ras[0:r, :, :] if s.sample else (
                    t_rap[:, s.tile, :, :] if s.fixed else
                    t_rap[:, bass.ds(s.tile, 1), :, :].rearrange("p o c d -> p (o c) d"))
                n, half = A_HEADS + A_KV, ROT // 2
                x = land[0:r, b, 0:n * A_DIM].rearrange("p (h d) -> p h d", d=A_DIM)
                xa, xb = x[:, :, 0:half], x[:, :, half:ROT]
                cos = tab[:, 0, :].unsqueeze(1).broadcast_to([r, n, half])
                sin = tab[:, 1, :].unsqueeze(1).broadcast_to([r, n, half])
                V.tensor_tensor(rp1[0:r, :, 0, :], xa, cos, ALU.mult)
                V.tensor_tensor(rp1[0:r, :, 1, :], xb, cos, ALU.mult)
                V.tensor_tensor(rp2[0:r, :, 0, :], xa, sin, ALU.mult)
                ch(V.tensor_tensor(rp2[0:r, :, 1, :], xb, sin, ALU.mult))
                V.tensor_tensor(xa, rp1[0:r, :, 0, :], rp2[0:r, :, 1, :], ALU.subtract)
                V.tensor_tensor(xb, rp1[0:r, :, 1, :], rp2[0:r, :, 0, :], ALU.add).then_inc(a_qk, 1)
                ch.end()

            def a_lo(L, s):
                v.wait_ge(qk_hi, tn(L, s) + 1)
                q, k = (land[:, s.par, o:o + w].rearrange("p (h d) -> p h d", d=A_DIM)
                        for o, w in ((0, A_W), (A_W, KV_W)))
                V.scalar_tensor_tensor(out=q16[:, :, 1, :], in0=q, scalar=qk_s[:, 0:1], in1=q16[:, :, 0, :],
                                       op0=ALU.mult, op1=ALU.subtract)
                kh, kl = (k16[:, o:o + A_KV * w].rearrange("p (g d) -> p g d", d=w)[:, :, 0:A_DIM]
                          for o, w in ((0, P), (A_KV * P, A_DIM)))
                V.scalar_tensor_tensor(out=kl, in0=k, scalar=qk_s[:, 1:2], in1=kh,
                                       op0=ALU.mult, op1=ALU.subtract).then_inc(qk_lo, 1)

            def gate(ph, L, s, p, n, col):
                r, b = s.rows, lpar(ph, s)
                v.wait_ge(act_piece, apiece(ph, L, s, 2) + 1)
                th = land[0:r, b, col:col + n]
                V.scalar_tensor_tensor(out=th, in0=th, scalar=1.0, in1=bank(ph, s, p)[0:r, 512 - n:512],
                                       op0=ALU.add, op1=ALU.mult).then_inc(dve_piece, 1)

            def a_vcopy(L, s):
                if s.sample:
                    V.memset(v16[:, 0, :, :], 0.0)
                    return
                ch = Chain(v, ch_v, 1, tn(L, s))
                x, d = land[:, s.par, A_W + KV_W:A_W + 2 * KV_W], cs["A"][:, 2:3]
                ch(V.tensor_scalar(v16[:, s.par, 0, :], x, d, None, ALU.mult))
                V.scalar_tensor_tensor(out=v16[:, s.par, 1, :], in0=x, scalar=d, in1=v16[:, s.par, 0, :],
                                       op0=ALU.mult, op1=ALU.subtract)
                ch.end()

            def a_plo(L, s, g):
                if s.sample:
                    return
                v.wait_ge(a_po, 2 * an(L, s) + g + 1)
                for q in range(2):
                    c = slice(q * 512, (q + 1) * 512)
                    last = V.scalar_tensor_tensor(out=pT16[:, 1, c], in0=XX[q][:, :], scalar=P_TOP,
                                                  in1=pT16[:, 0, c], op0=ALU.mult, op1=ALU.subtract)
                last.then_inc(a_pl, 1)

            def a_softmax(L, s, g):
                n = 2 * an(L, s) + g
                ch = Chain(v, ch_asm, 3, 2 * L + g) if s.sample else Chain(v, ch_asp, 2, 2 * tn(L, s) + g)
                alone(v, a_s, n + 1)
                if s.sample:
                    parts = ((S0[:, :], 0, 512), (S1[:, :], 512, 512), (TK[:, 0:NS], KEYS, NS))
                    for q, (src, o, w) in enumerate(parts):
                        last = V.tensor_tensor_reduce(
                            out=prob[:, o:o + w], in0=src, in1=t_ms[:, o:o + w].bitcast(BF16), scale=1.0,
                            scalar=-3e38,
                            op0=ALU.add, op1=ALU.max, accum_out=mr[:, g, q:q + 1])
                    ch(last)
                    ch(V.tensor_reduce(rt[:, 0:1], mr[:, g, 0:3], AX.X, ALU.max))
                    ch(V.scalar_tensor_tensor(out=nm[:, g, 0:1], in0=rt[:, 0:1], scalar=-(A_DIM ** -0.5),
                                              in1=nsks[:, g:g + 1], op0=ALU.mult, op1=ALU.min))
                    V.tensor_tensor(sd[:, g, 0:1], nm[:, g, 0:1], sks[:, g:g + 1], ALU.add).then_inc(a_sm, 1)
                else:
                    m = t_ma[:, 2 if s.first else s.par, :].bitcast(BF16)
                    for h in range(A_GROUP):
                        last = V.tensor_tensor_reduce(
                            out=prob[:, h * 256:(h + 1) * 256], in0=SS[h // 2][:, (h % 2) * 256:(h % 2) * 256 + 256],
                            in1=m, scale=1.0, scalar=-3e38, op0=ALU.add, op1=ALU.max,
                            accum_out=mr[:, g, h:h + 1])
                    ch(last)
                    gs = slice(g * A_GROUP, (g + 1) * A_GROUP)
                    ch(V.scalar_tensor_tensor(out=nm[:, g, :], in0=mr[:, g, :], scalar=unqk[:, 1:2],
                                              in1=nsk[:, gs], op0=ALU.mult, op1=ALU.min))
                    V.tensor_tensor(sd[:, g, :], nm[:, g, :], sk[:, gs], ALU.add).then_inc(a_sm, 1)
                ch.end()

            def a_mix(L, s, g):
                n, b = 2 * an(L, s) + g, s.par
                ch = Chain(v, ch_amx, 3, n)
                w = 1 if s.sample else A_GROUP
                v.wait_ge(a_ex, n + 1)
                ch(V.tensor_tensor(rr[:, g, 0:w], rsum[:, g, 0:w], es[:, g, 0:w], ALU.add))
                ch(V.reciprocal(rr[:, g, 0:w], rr[:, g, 0:w]))
                back = cs["A"][:, 1:2] if s.sample else cs["A"][:, 3:4]
                ch(V.tensor_scalar(rr[:, g, 0:w], rr[:, g, 0:w], back, None, ALU.mult))
                v.wait_ge(a_pv, n + 1)
                if g == 0:
                    v.wait_ge(mix_out[b], 16 * mix_count("A", L, s))
                th0 = A_W + 2 * KV_W + g * A_GROUP * A_DIM
                if s.sample:
                    tmp = kts[0:NS, 0:A_GROUP * A_DIM]
                    for h in range(A_GROUP):
                        q = slice(h * NS, (h + 1) * NS)
                        last = V.tensor_scalar(tmp[:, h * A_DIM:(h + 1) * A_DIM], OB[q, 0:A_DIM],
                                               rr[q, g, 0:1], None, ALU.mult)
                    last.then_inc(ch_ams, 1)
                    v.wait_ge(ch_ams, 2 * L + g + 1)
                    V.tensor_tensor(mix[0:NS, b, g * 256:(g + 1) * 256], tmp, land[0:NS, b, th0:th0 + 256],
                                    ALU.mult).then_inc(a_mx, 1)
                else:
                    for h in range(A_GROUP):
                        o = h * A_DIM
                        last = V.scalar_tensor_tensor(
                            out=mix[:, b, g * 256 + o:g * 256 + o + A_DIM], in0=OB[:, o:o + A_DIM],
                            scalar=rr[:, g, h:h + 1], in1=land[:, b, th0 + o:th0 + o + A_DIM],
                            op0=ALU.mult, op1=ALU.mult)
                    last.then_inc(a_mx, 1)
                ch.end()

            def b_rope(ph, L, s):
                r, b = s.rows, lpar(ph, s)
                v.wait_ge(pe_piece, piece(ph, L, s, 0) + 1)
                tab = t_rbs[0:r, :, :] if s.sample else (
                    t_rbp[:, s.tile, :, :] if s.fixed else
                    t_rbp[:, bass.ds(s.tile, 1), :, :].rearrange("p o c d -> p (o c) d"))
                src = bank(ph, s, 0)[0:r, :].rearrange("p (g d) -> p g d", d=DK // 2)
                for out, i in ((t1, 0), (t2, 1)):
                    last = V.scalar_tensor_tensor(
                        out=out[0:r, :].rearrange("p (g d) -> p g d", d=DK // 2), in0=src,
                        scalar=cs[ph][0:r, 0:1], in1=tab[:, i, :].unsqueeze(1).broadcast_to([r, 8, DK // 2]),
                        op0=ALU.mult, op1=ALU.mult)
                last.then_inc(dve_piece, 1)
                v.wait_ge(dve_piece, piece(ph, L, s, 0) + 2)
                a, c = (t[0:r, :].rearrange("p (g c d) -> p g c d", c=2, d=DK // 2) for t in (t1, t2))
                o = land[0:r, b, 0:512].rearrange("p (g c d) -> p g c d", c=2, d=DK // 2)
                V.tensor_tensor(o[:, :, 0, :], a[:, :, 0, :], c[:, :, 1, :], ALU.subtract)
                V.tensor_tensor(o[:, :, 1, :], a[:, :, 1, :], c[:, :, 0, :], ALU.add).then_inc(b_qk, 1)

            def b_decay(ph, L, s):
                v.wait_ge(b_st, bn(ph, L, s) + 1)
                h = 2 * hb(ph)
                if s.sample:
                    out = stm[0:NS, 0:2 * NS].rearrange("p (h n) -> p h n", h=2)
                    src = S0[0:NS, 0:2 * NS].rearrange("p (h n) -> p h n", h=2)
                    V.tensor_tensor(out, src, t_decs[:, h:h + 2, :], ALU.mult).then_inc(b_dm, 1)
                else:
                    V.tensor_tensor(stm, S0[:, 0:256], t_dec[:, h:h + 2, :].rearrange("p h n -> p (h n)"),
                                    ALU.mult).then_inc(b_dm, 1)

            def b_vbd(ph, L, s):
                v.wait_ge(act_piece, apiece(ph, L, s, 1) + 1)
                b = lpar(ph, s)
                for h in range(2):
                    x = vd[0:NS, b, h * P:(h + 1) * P].unsqueeze(1).broadcast_to([NS, DEC_BATCH, P])
                    m = t_cols[0:NS, 24:32].unsqueeze(2).broadcast_to([NS, DEC_BATCH, P])
                    last = V.tensor_tensor(vbd[0:NS, h, :, :], x, m, ALU.mult)
                last.then_inc(b_vb, 1)

            def b_state(ph, L, s):
                v.wait_ge(b_o, bn(ph, L, s) + 1)
                st, h0 = state[hb(ph)], 2 * hb(ph)
                if s.sample:
                    for h in range(2):
                        for q, bk in enumerate(((S1, X0), (X1, S0))[h]):
                            x = stS[:, h, 4 * q:4 * q + 4, :]
                            V.scalar_tensor_tensor(out=x, in0=x, scalar=lam(h0 + h) ** DEC_SEQ,
                                                   in1=bk[:, :].rearrange("p (b v) -> p b v", v=DV),
                                                   op0=ALU.mult, op1=ALU.add)
                    v.wait_ge(st_out, (L + 1) * 64)
                    V.memset(st, 0.0).then_inc(b_su, 1)
                else:
                    for h in range(2):
                        x = st[:, h * P:(h + 1) * P]
                        last = V.scalar_tensor_tensor(out=x, in0=x, scalar=lam(h0 + h) ** P,
                                                      in1=S1[:, h * P:(h + 1) * P], op0=ALU.mult, op1=ALU.add)
                    last.then_inc(b_su, 1)

            def b_mix(ph, L, s):
                r, n, b = s.rows, bn(ph, L, s), lpar(ph, s)
                ch = Chain(v, ch_bo, 4 + RSQRT_LINKS, n)
                h0, cc = 2 * hb(ph), 12 if s.sample else 0
                v.wait_ge(b_sq, n + 1)
                ch(V.tensor_tensor(oms[0:r, :], oss[0:r, :], t_cols[0:r, cc + h0:cc + h0 + 2], ALU.mult))
                ch(V.tensor_scalar(oms[0:r, :], oms[0:r, :], EPS, None, ALU.add))
                rsqrt(ch, oms[0:r, :], oy[0:r, :], ot[0:r, :])
                ch(V.tensor_tensor(oy[0:r, :], oy[0:r, :], t_cols[0:r, cc + 4 + h0:cc + 6 + h0], ALU.mult))
                ch(V.tensor_scalar(oy[0:r, :], oy[0:r, :], cs[ph][0:r, 1:2], None, ALU.mult))
                v.wait_ge(mix_out[b], 16 * mix_count(ph, L, s))
                for h in range(2):
                    c = slice(h * P, (h + 1) * P)
                    last = V.scalar_tensor_tensor(out=mix[0:r, b, c], in0=OB[0:r, c], scalar=oy[0:r, h:h + 1],
                                                  in1=land[0:r, b, 768 + h * P:768 + (h + 1) * P],
                                                  op0=ALU.mult, op1=ALU.mult)
                last.then_inc(b_mx, 1)
                ch.end()

            def o_scale(L, s):
                r, b = s.rows, s.par
                ch = Chain(v, ch_om, 2, L * STEPS + s.v)
                v.wait_ge(mx_ld[b], 16 * (L * (9 - b) + s.half + 1))
                ch(V.tensor_reduce(mq[0:r, :], mxt[0:r, b, :], AX.X, ALU.max, apply_absolute_value=True))
                ch(V.tensor_scalar(mqq[0:r, b:b + 1], mq[0:r, :], TOP, TINY, ALU.mult, ALU.max))
                V.reciprocal(minv[0:r, b:b + 1], mqq[0:r, b:b + 1]).then_inc(o_sc, 1)
                ch.end()

            def o_unscale(L, s):
                r, b = s.rows, s.par
                ch = Chain(v, ch_ou, 1, L * STEPS + s.v)
                ch(V.tensor_scalar(mdd[0:r, b:b + 1], mqq[0:r, b:b + 1], cs["O"][0:r, 0:1], None, ALU.mult))
                ch.end()

            def lo(ready, n, banks, r, dst):
                for q, bk in enumerate(banks):
                    v.wait_ge(ready, n + q + 1)
                    src = bk[:, :].rearrange("p (k t) -> p k t", t=P)[:, :, 0:r]
                    last = V.tensor_tensor(dst(1, q), src, dst(0, q), ALU.subtract)
                return last

            def o_mlo(L, s):
                m = mT[s.par]
                lo(o_hi, 2 * (L * STEPS + s.v), m_banks(s), s.rows,
                   lambda e, q: m[:, 4 * q:4 * q + 4, e, 0:s.rows]).then_inc(o_lo, 1)

            def h_lo_part(L, s):
                lo(h_hi, 2 * hn(L, s), h_banks(L, s), s.rows,
                   lambda e, q: hT[:, e, 4 * q:4 * q + 4, hcols(s)]).then_inc(h_lo, 1)

            def o_add(L, s, p):
                r, b = s.rows, s.par
                v.wait_ge(pe_piece, piece("O", L, s, p) + 1)
                if p == 0:
                    v.wait_ge(x_ld[b], 16 * (L * (9 - b) + s.half + 1))
                x = xt_[0:r, b, p * 512:(p + 1) * 512]
                V.scalar_tensor_tensor(out=x, in0=bank("O", s, p)[0:r, :], scalar=mdd[0:r, b:b + 1], in1=x,
                                       op0=ALU.mult, op1=ALU.add).then_inc(dve_piece, 1)

            def h_rstd(L, s):
                r, b = s.rows, s.par
                ch = Chain(v, ch_h, 1 + RSQRT_LINKS, L * STEPS + s.v)
                v.wait_ge(h_sq, hn(L, s) + 1)
                ch(V.tensor_scalar(xms[0:r, 0:1], xss[0:r, 0:1], 1.0 / D_MODEL, EPS, ALU.mult, ALU.add))
                y = xy[0:r, b:b + 1]
                rsqrt(ch, xms[0:r, 0:1], y, xt[0:r, 0:1])
                V.tensor_scalar(y, y, H_SCALE, None, ALU.mult).then_inc(h_rs, 1)
                ch.end()

            def h_rstd_pair(j):
                r, cols = (NS, slice(0, 1)) if j == 0 else (P, slice(0, 2))
                ch = Chain(v, ch_p, 1 + RSQRT_LINKS, j)
                v.wait_ge(h_sq, 2 * j + 1)
                ch(V.tensor_scalar(xms[0:r, cols], xss[0:r, cols], 1.0 / D_MODEL, EPS, ALU.mult, ALU.add))
                y = xy[0:r, 2 * (j % 2) + cols.start:2 * (j % 2) + cols.stop]
                rsqrt(ch, xms[0:r, cols], y, xt[0:r, cols])
                V.tensor_scalar(y, y, H_SCALE, None, ALU.mult).then_inc(h_rs, 1 if j == 0 else 2)
                ch.end()

            def w_convert(kind, k, n0):
                ch = Chain(v, ch_wd, 3 * len(CH[kind]), n0)
                for c, (_, n) in enumerate(CH[kind]):
                    t = w_tmp2[:, 0:n]
                    ch(V.tensor_scalar(t, raw(kind, k, c), w_gs[:, k:k + 1], None, ALU.mult))
                    ch(V.tensor_copy(w16(kind, k, c, 0), t))
                    ch(V.tensor_tensor(w16(kind, k, c, 1), t, w16(kind, k, c, 0), ALU.subtract))
                ch.end()

            E = Step(STEPS - 1)
            v.sem_inc(dve_piece, 1)
            V.memset(ones[:, :], 1.0)
            V.memset(r2[:, :], 0.0).then_inc(init, 1)
            v.wait_ge(init, 1)
            v.wait_ge(id_ld, ID_LOADS * 16)
            V.tensor_copy(eye16[:, :], eye[:, :])
            V.memset(kT_hi[:, :, :, :], 0.0)
            V.memset(kT_lo[:, :, :, :], 0.0)
            w_gain(0).then_inc(ch_l, 1)
            v.wait_ge(ch_l, 1)

            PAIRS = TILES // 2
            h_rstd_pair(0)
            h_rstd_pair(1)
            for j in range(1, PAIRS + 1):
                if j < PAIRS:
                    h_rstd_pair(j + 1)
                if j == 3:
                    w_scale(0, "A")
                h_lo_part(-1, Step(2 * j - 2))
                h_lo_part(-1, Step(2 * j - 1))
                if j in (1, 2):
                    w_absmax(0, "A", j - 1)
                if j > PAIRS - DVE_KT:
                    w_convert("A", KT - PAIRS + j - 1, j - 1 - PAIRS + DVE_KT)
            h_lo_part(-1, E)
            v.wait_ge(c_ld, CONST_LOADS * 16)

            def layer(L, last):
                V.tensor_copy(qk_g[:, :, :], qk_all[:, bass.ds(L, 1), :, :].rearrange("p o c d -> p (o c) d"))
                V.tensor_copy(sk[:, :], sk_all[:, bass.ds(L, 1), :].rearrange("p o k -> p (o k)"))
                V.tensor_scalar(nsk[:, :], sk_all[:, bass.ds(L, 1), :].rearrange("p o k -> p (o k)"), -1.0,
                                None, ALU.mult)
                V.tensor_copy(sks[:, :], sks_all[:, bass.ds(L, 1), :].rearrange("p o k -> p (o k)"))
                V.tensor_scalar(nsks[:, :], sks_all[:, bass.ds(L, 1), :].rearrange("p o k -> p (o k)"), -1.0,
                                None, ALU.mult).then_inc(ch_l, 1)
                v.wait_ge(ch_l, L * 2 + 2)
                ch = Chain(v, ch_g, 6, L)
                ch(V.tensor_reduce(g_mx[:, :], qk_g[:, :, :], AX.X, ALU.max, apply_absolute_value=True))
                ch(V.tensor_scalar(g_mx[:, :], g_mx[:, :], GAIN_MIN, None, ALU.max))
                ch(V.reciprocal(qk_s[:, :], g_mx[:, :]))
                ch(V.tensor_scalar(qk_s[:, :], qk_s[:, :], QK_TOP, None, ALU.mult))
                ch(V.tensor_scalar(unqk[:, 0:1], g_mx[:, 0:1], g_mx[:, 1:2], A_DIM ** -0.5 / QK_TOP ** 2,
                                   ALU.mult, ALU.mult))
                ch(V.tensor_scalar(unqk[:, 1:2], unqk[:, 0:1], -1.0, None, ALU.mult))
                ch.end()

                def a_step(s):
                    a_land_q(L, s)
                    if not (s.fixed and s.c < 2):
                        a_plo(L, s - 2, 1)
                    if not s.sample:
                        a_softmax(L, s - 1, 0)
                    if not (s.fixed and s.c < 2):
                        a_mix(L, s - 2, 1)
                    if not s.sample:
                        a_vcopy(L, s - 1)
                    ch = a_land_k(L, s)
                    if not s.sample:
                        a_softmax(L, s - 1, 1)
                    a_rotate(L, s, ch)
                    if not s.sample:
                        a_plo(L, s - 1, 0)
                        a_lo(L, s)
                    gate("A", L, s, 2, A_W, A_W + 2 * KV_W)
                    if not s.sample:
                        a_mix(L, s - 1, 0)

                for c in range(5):
                    a_step(Step(c))
                    if c in (2, 3):
                        w_absmax(L, "B0", c - 2)
                    if c == 4:
                        w_scale(L, "B0")
                with v.Fori(0, 6) as i:
                    for c in (5, 6):
                        a_step(Step(c, i))

                s = Step(0)
                a_plo(L, E - 1, 1)
                a_mix(L, E - 1, 1)
                a_vcopy(L, E)
                a_softmax(L, E, 0)
                V.memset(r1[:, 2048:2048 + 2 * 288], 0.0)
                b_rope("B0", L, s)
                a_plo(L, E, 0)
                a_softmax(L, E, 1)
                gate("B0", L, s, 1, 256, 768)
                a_mix(L, E, 0)
                s = Step(1)
                b_rope("B0", L, s)
                a_plo(L, E, 1)
                b_decay("B0", L, Step(0))
                a_mix(L, E, 1)
                b_vbd("B0", L, Step(0))
                gate("B0", L, s, 1, 256, 768)
                b_state("B0", L, Step(0))
                b_mix("B0", L, Step(0))

                def b_old(ph, s):
                    b_state(ph, L, s)
                    b_mix(ph, L, s)

                def b_step(ph, s):
                    if s.fixed and s.c == 1:
                        b_vbd(ph, L, s - 1)
                    b_decay(ph, L, s - 1)
                    b_rope(ph, L, s)
                    b_old(ph, s - 1)
                    gate(ph, L, s, 1, 256, 768)

                for ph, lo_c, nxt in (("B0", 2, "B1"), ("B1", 1, "O")):
                    if ph == "B1":
                        b_decay("B0", L, E)
                        b_rope("B1", L, Step(0))
                        b_old("B0", E)
                        gate("B1", L, Step(0), 1, 256, 768)
                    for c in range(lo_c, 5):
                        b_step(ph, Step(c))
                        if c in (2, 3):
                            w_absmax(L, nxt, c - 2)
                        if c == 4:
                            w_scale(L, nxt)
                    with v.Fori(0, 6 - hb(ph)) as i:
                        for c in (5, 6):
                            b_step(ph, Step(c, i))
                b_step("B1", E - 1)
                for c in range(2):
                    o_scale(L, Step(c))
                    o_unscale(L, Step(c))
                b_step("B1", E)

                o_mlo(L, Step(0))
                b_decay("B1", L, E)
                o_add(L, Step(0), 0)
                b_old("B1", E)
                o_add(L, Step(0), 1)
                o_mlo(L, Step(1))
                o_scale(L, Step(2))

                def o_step(s):
                    if not last:
                        h_rstd(L, s - 1)
                    if not (s.fixed and s.c == STEPS - 1):
                        v.wait_ge(dve_piece, piece("O", L, s - 1, 1) + 2)
                        o_unscale(L, s + 1)
                        o_mlo(L, s + 1)
                    if not (s.fixed and s.c >= STEPS - 2):
                        o_scale(L, s + 2)
                    o_add(L, s, 0)
                    if not last:
                        h_lo_part(L, s - 1)
                    o_add(L, s, 1)

                for c in range(1, 5):
                    o_step(Step(c))
                    if last:
                        continue
                    if c == 2:
                        w_gain(L + 1).then_inc(ch_l, 1)
                        v.wait_ge(ch_l, L * 2 + 3)
                        w_absmax(L + 1, "A", 0)
                    if c == 3:
                        w_absmax(L + 1, "A", 1)
                    if c == 4:
                        w_scale(L + 1, "A")
                with v.Fori(0, 5) as i:
                    for c in (5, 6):
                        o_step(Step(c, i))
                o_step(E - 1)
                o_step(E)
                if not last:
                    h_rstd(L, E)
                    h_lo_part(L, E)

            with v.Fori(0, DEPTH - 1) as L:
                layer(L, False)
            layer(DEPTH - 1, True)

        @block.scalar
        def _(act):
            A = nc.scalar

            def a_q(L, s):
                r = s.rows
                act.wait_ge(pe_piece, piece("A", L, s, 0) + 1)
                A.activation(sq[0:r, 0:A_W], bank("A", s, 0)[0:r, :], ACT.Square,
                             scale=cs["A"][0:r, 0:1]).then_inc(act_piece, 1)

            def a_kv(L, s):
                r, b, c = s.rows, s.par, cs["A"]
                act.wait_ge(pe_piece, piece("A", L, s, 1) + 1)
                if s.fixed and s.c == 2:
                    act.wait_ge(kvs_out, (L + 1) * 256)
                    act.wait_ge(a_pv, 2 * L * STEPS + 2)
                src = bank("A", s, 1)
                A.activation(sq[0:r, A_W:A_W + KV_W], src[0:r, 0:KV_W], ACT.Square, scale=c[0:r, 0:1])
                A.activation(land[0:r, b, A_W + KV_W:A_W + 2 * KV_W], src[0:r, KV_W:2 * KV_W], ACT.Copy,
                             scale=c[0:r, 0:1]).then_inc(act_piece, 1)

            def a_tanh(L, s):
                r = s.rows
                act.wait_ge(pe_piece, piece("A", L, s, 2) + 1)
                A.activation(land[0:r, s.par, A_W + 2 * KV_W:], bank("A", s, 2)[0:r, :], ACT.Tanh,
                             scale=cs["A"][0:r, 1:2]).then_inc(act_piece, 1)

            def a_tout(L, s):
                act.wait_ge(a_tk, an(L, s) + 1)
                if s.sample:
                    A.activation(qT[0:A_DIM, 0:A_HEADS * NS], TK[0:A_DIM, 0:A_HEADS * NS], ACT.Copy)
                    A.activation(knew[0:A_DIM, :, :].rearrange("p g n -> p (g n)"),
                                 TK[0:A_DIM, A_HEADS * NS:(A_HEADS + A_KV) * NS], ACT.Copy)
                    last = cached_keys_out()
                else:
                    S16 = S0[:, :].bitcast(F16).rearrange("p (q t) -> p q t", t=P)
                    A.activation(kT_hi[:, :, s.par, :], S16[:, 0:2, :], ACT.Copy)
                    A.activation(kT_lo[:, :, s.par, :], S16[0:A_DIM, 2:4, :], ACT.Copy)
                    last = A.activation(qT16, TK[:, :].bitcast(F16), ACT.Copy)
                last.then_inc(a_te, 1)

            def a_hi(L, s):
                act.wait_ge(a_qk, an(L, s) + 1)
                q, k = (land[:, s.par, o:o + w].rearrange("p (h d) -> p h d", d=A_DIM)
                        for o, w in ((0, A_W), (A_W, KV_W)))
                A.activation(q16[:, :, 0, :], q, ACT.Copy, scale=qk_s[:, 0:1])
                kh = k16[:, 0:A_KV * P].rearrange("p (g d) -> p g d", d=P)
                for e in range(2):
                    last = A.activation(kh[:, :, e * A_DIM:(e + 1) * A_DIM], k, ACT.Copy, scale=qk_s[:, 1:2])
                last.then_inc(qk_hi, 1)

            def cached_keys_out():
                for q in range(2):
                    last = A.activation(kts[0:A_DIM, q * 512:(q + 1) * 512], XX[q][0:A_DIM, :], ACT.Copy)
                return last

            def a_exp(L, s, g):
                act.wait_ge(a_sm, 2 * an(L, s) + g + 1)
                if s.sample:
                    A.activation(prob[:, :], prob[:, :], ACT.Exp, scale=A_DIM ** -0.5, bias=nm[:, g, 0:1],
                                 accum_out=rsum[:, g, 0:1])
                else:
                    for h in range(A_GROUP):
                        x = prob[:, h * 256:(h + 1) * 256]
                        A.activation(x, x, ACT.Exp, scale=unqk[:, 0:1], bias=nm[:, g, h:h + 1],
                                     accum_out=rsum[:, g, h:h + 1])
                w = 1 if s.sample else A_GROUP
                A.activation(es[:, g, 0:w], sd[:, g, 0:w], ACT.Exp).then_inc(a_ex, 1)

            def a_pout(L, s, g):
                act.wait_ge(a_pt, 2 * an(L, s) + g + 1)
                for q in range(2):
                    c = slice(q * 512, (q + 1) * 512)
                    if s.sample:
                        A.activation(pT[:, c], XX[q][:, :], ACT.Copy)
                    else:
                        last = A.activation(pT16[:, 0, c], XX[q][:, :], ACT.Copy, scale=P_TOP)
                if s.sample:
                    last = A.activation(pT[0:NS, KEYS:KEYS + P], TK[0:NS, P:2 * P], ACT.Copy)
                last.then_inc(a_po, 1)

            def b_vg(ph, L, s):
                r, b, c = s.rows, lpar(ph, s), cs[ph]
                act.wait_ge(pe_piece, piece(ph, L, s, 1) + 1)
                if ph == "B0" and s.fixed and s.c == 1:
                    act.wait_ge(kv_out, (L + 1) * 32)
                src = bank(ph, s, 1)
                A.activation(land[0:r, b, 512:768], src[0:r, 0:256], ACT.Copy, scale=c[0:r, 0:1])
                k = 4 if s.sample else 2
                for h in range(2):
                    A.activation(vd[0:r, b, h * P:(h + 1) * P], src[0:r, h * P:(h + 1) * P], ACT.Copy,
                                 scale=c[0:r, k + h:k + h + 1])
                A.activation(land[0:r, b, 768:1024], src[0:r, 256:512], ACT.Tanh,
                             scale=c[0:r, 1:2]).then_inc(act_piece, 1)

            def b_tout(ph, L, s):
                act.wait_ge(b_tk, bn(ph, L, s) + 1)
                if s.sample:
                    A.activation(qkT[:, 0:4 * NS], TK[:, 0:4 * NS], ACT.Copy)
                    for h in range(2):
                        last = A.activation(
                            qtm[:, h, :].rearrange("p (b x) -> p b x", x=NS + DEC_SEQ)[:, :, 0:DEC_SEQ],
                            TK[:, h * NS:(h + 1) * NS].rearrange("p (b x) -> p b x", x=DEC_SEQ), ACT.Copy)
                else:
                    last = A.activation(qkT[:, :], TK[:, :], ACT.Copy)
                last.then_inc(b_te, 1)

            def b_squares(ph, L, s):
                r = s.rows
                act.wait_ge(b_o, bn(ph, L, s) + 1)
                for h in range(2):
                    last = A.activation(osq[0:r, h * P:(h + 1) * P], OB[0:r, h * P:(h + 1) * P], ACT.Square,
                                        accum_out=oss[0:r, h:h + 1])
                last.then_inc(b_sq, 1)

            def o_mscale(L, s):
                r, b, n = s.rows, s.par, L * STEPS + s.v
                act.wait_ge(o_sc, n + 1)
                if not s.sample:
                    act.wait_ge(o_tm, n)
                A.activation(msc[0:r, :], mxt[0:r, b, :], ACT.Copy, scale=minv[0:r, b:b + 1]).then_inc(o_ms, 1)

            def hi(banks, r, dst, ready):
                for q, bk in enumerate(banks):
                    src = bk[:, :].rearrange("p (k t) -> p k t", t=P)[:, :, 0:r]
                    A.activation(dst(q), src, ACT.Copy).then_inc(ready, 1)

            def o_mhi(L, s):
                act.wait_ge(o_tm, L * STEPS + s.v + 1)
                m = mT[s.par]
                hi(m_banks(s), s.rows, lambda q: m[:, 4 * q:4 * q + 4, 0, 0:s.rows], o_hi)

            def h_squares(L, s):
                r = s.rows
                if pro(L):
                    act.wait_ge(x4_ld[s.ring], 16 * (s.turn + 1))
                    x, out, col = x4[0:r, s.ring, :], xsq, 0 if s.par or s.sample else 1
                    if not s.sample:
                        act.wait_ge(h_sq, s.v)
                else:
                    act.wait_ge(dve_piece, piece("O", L, s, 1) + 2)
                    x, out, col = xt_[0:r, s.par, :], xn, 0
                    act.wait_ge(h_t, hn(L, s))
                A.activation(out[0:r, :], x, ACT.Square, accum_out=xss[0:r, col:col + 1]).then_inc(h_sq, 1)

            def h_norm(L, s):
                r, col = s.rows, s.par
                x = xt_[0:r, s.par, :]
                if pro(L):
                    x, col = x4[0:r, s.ring, :], 0 if s.sample else (2, 3, 0, 1)[(s.c - 1) % 4]
                    if not (s.fixed and s.c < 2):
                        act.wait_ge(h_t, s.v - 1)
                act.wait_ge(h_rs, hn(L, s) + 1)
                A.activation(xn_of(L, s)[0:r, :], x, ACT.Copy, scale=xy[0:r, col:col + 1]).then_inc(h_xn, 1)

            def h_hi_part(L, s):
                act.wait_ge(h_t, hn(L, s) + 1)
                hi(h_banks(L, s), s.rows, lambda q: hT[:, 0, 4 * q:4 * q + 4, hcols(s)], h_hi)

            E = Step(STEPS - 1)
            act.wait_ge(init, 1)

            def pair(a, b, before, following=()):
                h_norm(-1, a)
                for s in following:
                    h_squares(-1, s)
                h_hi_part(-1, before)
                h_norm(-1, b)
                h_hi_part(-1, a)

            h_squares(-1, early(0))
            h_norm(-1, early(0))
            h_squares(-1, early(1))
            h_squares(-1, early(2))
            pair(early(1), early(2), early(0), (early(3), early(4)))
            with act.Fori(0, (STEPS - 5) // 4) as i:
                for c in (3, 5):
                    pair(early(c, i), early(c + 1, i), early(c - 1, i), (early(c + 2, i), early(c + 3, i)))
            pair(early(STEPS - 2), early(STEPS - 1), early(STEPS - 3))
            h_hi_part(-1, E)
            def layer(L, last):
                def a_step(s):
                    tail, old = not s.sample, not (s.fixed and s.c < 2)
                    late = old and not (s - 2).sample
                    if old and not late:
                        a_pout(L, s - 2, 1)
                    if tail:
                        a_tout(L, s - 1)
                    if late:
                        a_pout(L, s - 2, 1)
                    a_q(L, s)
                    a_kv(L, s)
                    if tail:
                        a_exp(L, s - 1, 0)
                        if (s - 1).sample:
                            act.wait_ge(s_ct, L + 1)
                            cached_keys_out().then_inc(s_ce, 1)
                        a_pout(L, s - 1, 0)
                        a_exp(L, s - 1, 1)
                        a_hi(L, s)
                    a_tanh(L, s)

                for c in range(3):
                    a_step(Step(c))
                with act.Fori(0, (STEPS - 3) // 2) as i:
                    for c in (3, 4):
                        a_step(Step(c, i))
                a_tout(L, E)
                a_pout(L, E - 1, 1)
                a_exp(L, E, 0)
                a_pout(L, E, 0)
                b_vg("B0", L, Step(0))
                a_exp(L, E, 1)
                b_tout("B0", L, Step(0))
                a_pout(L, E, 1)
                b_vg("B0", L, Step(1))
                b_squares("B0", L, Step(0))

                def b_step(ph, s):
                    b_tout(ph, L, s - 1)
                    b_squares(ph, L, s - 1)
                    b_vg(ph, L, s)

                for ph, lo_c in (("B0", 2), ("B1", 1)):
                    if ph == "B1":
                        b_tout("B0", L, E)
                        b_squares("B0", L, E)
                        b_vg("B1", L, Step(0))
                    for c in range(lo_c, 3):
                        b_step(ph, Step(c))
                    with act.Fori(0, (STEPS - 3) // 2 - hb(ph)) as i:
                        for c in (3, 4):
                            b_step(ph, Step(c, i))
                b_step("B1", E - 1)
                o_mscale(L, Step(0))
                b_step("B1", E)
                b_tout("B1", L, E)
                o_mhi(L, Step(0))
                o_mscale(L, Step(1))
                b_squares("B1", L, E)
                act.wait_ge(st_out, (L + 1) * 64 + 64)
                o_mhi(L, Step(1))
                o_mscale(L, Step(2))

                def o_step(s):
                    if not last:
                        h_squares(L, s - 1)
                    if not (s.fixed and s.c == STEPS - 1):
                        o_mhi(L, s + 1)
                    if not last:
                        h_norm(L, s - 1)
                    if not (s.fixed and s.c >= STEPS - 2):
                        o_mscale(L, s + 2)
                    if not last:
                        h_hi_part(L, s - 1)

                for c in range(1, 3):
                    o_step(Step(c))
                with act.Fori(0, (STEPS - 5) // 2) as i:
                    for c in (3, 4):
                        o_step(Step(c, i))
                o_step(E - 1)
                o_step(E)
                if not last:
                    h_squares(L, E)
                    h_norm(L, E)
                    h_hi_part(L, E)

            with act.Fori(0, DEPTH - 1) as L:
                layer(L, False)
            layer(DEPTH - 1, True)

        @block.gpsimd
        def _(pool):
            G = nc.gpsimd
            def convert(L, kind, done, kts=KT):
                alone(pool, w_max, wn(L, kind) + 1)
                G.partition_all_reduce(w_am[:, :], w_m1[:, :], P, bass.bass_isa.ReduceOp.max).then_inc(w_all, 1)
                pool.wait_ge(w_sc, wn(L, kind) + 1)
                ch = Chain(pool, ch_wp, 1, done * 3)
                for k in range(kts):
                    for c, (c0, n) in enumerate(CH[kind]):
                        g = w_gs[:, k:k + 1].broadcast_to([P, n])
                        t = w_tmp[:, 0:n]
                        ch(G.tensor_tensor(t, raw(kind, k, c), g, ALU.mult))
                        ch(G.tensor_tensor(w16(kind, k, c, 0), t, ones[:, 0:1].broadcast_to([P, n]), ALU.mult))
                        ch(G.tensor_tensor(w16(kind, k, c, 1), t, w16(kind, k, c, 0), ALU.subtract))
                pool.sem_inc(w_rd, 1)

            chunks = {k: KT * len(CH[k]) for k in BLOCKS}
            load_weights(G, "A", 0)
            for p in range(2):
                pool.sem_inc(mix_out[p], 16)
            pool.sem_inc(st_out, 64)
            convert(0, "A", 0, KT - DVE_KT)
            def layer(L, last):
                base = (KT - DVE_KT) * len(CH["A"]) + L * sum(chunks.values())
                for kind, after in (("B0", "A"), ("B1", "B0"), ("O", "B1"), ("A", "O"))[:3 if last else 4]:
                    nl = L + 1 if kind == "A" else L
                    pool.wait_ge(dve_piece, L * PIECES + PIECE0[after] + 1)
                    load_weights(G, kind, nl)
                    convert(nl, kind, base)
                    base = base + chunks[kind]

            with pool.Fori(0, DEPTH - 1) as L:
                layer(L, False)
            layer(DEPTH - 1, True)

        @block.sync
        def _(sp):
            def xs(s, prompt, sample):
                return sample if s.sample else (
                    prompt[s.col:s.col + P, :] if s.fixed else prompt[bass.ds(s.col, P), :])

            def load_x(L, s, prompt, sample):
                sp.dma_start(xt_[0:s.rows, s.par, :], xs(s, prompt, sample)).then_inc(x_ld[s.par], 16)

            def mixed_rows(s):
                return slice(s.col, s.col + s.rows) if s.fixed else bass.ds(s.col, P)

            def store_mix(ph, L, s):
                p = lpar(ph, s)
                if ph == "A":
                    sp.wait_ge(a_mx, 2 * an(L, s) + 2)
                    c0, n = 0, A_W
                else:
                    sp.wait_ge(b_mx, bn(ph, L, s) + 1)
                    c0, n = A_W + hb(ph) * 256, 256
                sp.dma_start(mixed[mixed_rows(s), c0:c0 + n], mix[0:s.rows, p, 0:n]).then_inc(mix_out[p], 16)

            def load_mixed(L, s):
                p = s.par
                sp.wait_ge(mix_out[p], 16 * mix_count("B1", L, s) + 16)
                sp.wait_ge(mix_out[1 - p], 16 * (L * MIX_OUT[1 - p] + MIX_OUT0["B1"][1 - p]) + 16)
                sp.dma_start(mxt[0:s.rows, p, :], mixed[mixed_rows(s), :]).then_inc(mx_ld[p], 16)

            def load_states(ph, L):
                for h in range(2):
                    src = state_ret[bass.ds(L, 1), :, 2 * hb(ph) + h, :, :].rearrange("o b k v -> k (o b) v")
                    sp.dma_start(stS[:, h, :, :], src).then_inc(sts_ld, 16)

            xp, ys = x_prompt[0], y_p[0]
            xsm, ysm = x_sample.rearrange("b t d -> (b t) d"), y_s.rearrange("b t d -> (b t) d")

            def load_early(s):
                sp.dma_start(x4[0:s.rows, s.ring, :], xs(s, xp, xsm)).then_inc(x4_ld[s.ring], 16)

            sp.dma_start(eye[:, :], ident).then_inc(id_ld, 16)
            with nc.allow_non_contiguous_dma(reason="small gains"):
                for l in range(DEPTH):
                    sp.dma_start(g_all[:, l, :], norm_g[l].rearrange("(k p) -> p k", p=P)).then_inc(id_ld, 16)
            for c in range(4):
                load_early(early(c))

            def next_early(s):
                sp.wait_ge(h_xn, s.v - 3)
                load_early(s)

            for c in range(4, 8):
                next_early(early(c))
            loads = [(t_cols[:, :], cols), (t_rap[:, :, :, :], rope_ap), (t_ras[:, :, :], rope_as),
                     (t_rbp[:, :, :, :], rope_bp), (t_rbs[:, :, :], rope_bs), (t_ma[:, :, :], mask_a),
                     (t_ms[:, :], mask_s), (t_dec[:, :, :], decay), (t_decs[:, :, :], decay_s)]
            for l in range(DEPTH):
                loads.append((qk_all[:, l, 0, :], q_g[l:l + 1, :].broadcast_to([P, A_DIM])))
                loads.append((qk_all[:, l, 1, :], k_g[l:l + 1, :].broadcast_to([P, A_DIM])))
                loads.append((sk_all[:, l, :], sinks[l:l + 1, :].broadcast_to([P, A_HEADS])))
                for h in range(A_HEADS):
                    g, q = h // A_GROUP, h % A_GROUP
                    loads.append((sks_all[q * NS:(q + 1) * NS, l, g:g + 1],
                                  sinks[l:l + 1, h:h + 1].broadcast_to([NS, 1])))
            assert len(loads) == CONST_LOADS
            with nc.allow_non_contiguous_dma(reason="small gains and sinks"):
                each = -(-len(loads) // (STEPS - 8))
                for c in range(8, STEPS):
                    next_early(early(c))
                    for dst, src in loads[(c - 8) * each:(c - 7) * each]:
                        sp.dma_start(dst, src).then_inc(c_ld, 16)
            sp.dma_start(ys, xp).then_inc(xy_cp, 16)
            sp.dma_start(ysm, xsm).then_inc(xy_cp, 16)
            for o, i in ((nk_s, cache_k), (nv_s, cache_v)):
                for l in range(DEPTH):
                    sp.dma_start(o[l, :, 0:WINDOW - DEC_SEQ].rearrange("b w g d -> b (w g d)"),
                                 i[l, :, DEC_SEQ:WINDOW].rearrange("b w g d -> b (w g d)")).then_inc(kc_out, 16)

            E = Step(STEPS - 1)
            def layer(L, last):
                def at(x):
                    return x[bass.ds(L, 1)]
                sp.wait_ge(h_lo, (L + 1) * STEPS)
                for dst, src in ((ck, cache_k), (cv, cache_v)):
                    sp.dma_start(dst, at(src).rearrange("o b w g d -> w (o b) (g d)")).then_inc(ckv_ld, 16)
                sp.wait_ge(a_qk, L * STEPS + 1)
                for o, c0 in ((nk_s, A_W), (nv_s, A_W + KV_W)):
                    for q in range(DEC_BATCH):
                        sp.dma_start(o[bass.ds(L, 1), q, WINDOW - DEC_SEQ:WINDOW].rearrange("o w g d -> (o w) (g d)"),
                                     land[q * DEC_SEQ:(q + 1) * DEC_SEQ, 0, c0:c0 + KV_W]).then_inc(kvs_out, 16)
                store_mix("A", L, Step(0))
                load_states("B0", L)
                store_mix("A", L, Step(1))
                store_mix("A", L, Step(2))
                with sp.Fori(0, (STEPS - 3) // 2) as i:
                    for c in (3, 4):
                        store_mix("A", L, Step(c, i))
                for o, c0 in ((nk_p, A_W), (nv_p, A_W + KV_W)):
                    sp.dma_start(at(o).rearrange("o n w g d -> (o n w) (g d)"),
                                 land[:, E.par, c0:c0 + KV_W]).then_inc(kv_out, 16)
                for ph in ("B0", "B1"):
                    for h in range(2):
                        sp.wait_ge(b_su, bn(ph, L, Step(0)) + 1)
                        dst = at(nst_s)[:, :, 2 * hb(ph) + h, :, :].rearrange("o b k v -> k (o b) v")
                        sp.dma_start(dst, stS[:, h, :, :]).then_inc(sts_out, 16)
                    if ph == "B0":
                        sp.wait_ge(sts_out, (L * 2 + 1) * 32)
                        load_states("B1", L)
                    for c in range(3):
                        store_mix(ph, L, Step(c))
                    if ph == "B1":
                        sp.wait_ge(sts_out, (L * 2 + 2) * 32)
                        for c in range(2):
                            load_mixed(L, Step(c))
                        sp.wait_ge(xy_cp, 32)
                        load_x(L, Step(0), ys, ysm)
                    with sp.Fori(0, (STEPS - 5) // 2) as i:
                        for c in (3, 4):
                            store_mix(ph, L, Step(c, i))
                    store_mix(ph, L, E - 1)
                    if ph == "B1":
                        sp.wait_ge(b_qk, (L + 1) * 2 * STEPS)
                        load_x(L, Step(1), ys, ysm)
                    sp.wait_ge(b_su, bn(ph, L, E) + 1)
                    for h in range(2):
                        sp.dma_start(at(nst_p)[:, 0, 2 * hb(ph) + h, :, :].rearrange("o k v -> (o k) v"),
                                     state[hb(ph)][:, h * P:(h + 1) * P]).then_inc(st_out, 16)
                    store_mix(ph, L, E)

                def next_mixed(s):
                    sp.wait_ge(o_ms, L * STEPS + s.v + 1)
                    load_mixed(L, s + 2)

                def o_step(s, loads=True, mixed_loads=True):
                    if mixed_loads:
                        next_mixed(s + 1)
                    sp.wait_ge(dve_piece, piece("O", L, s, 1) + 2)
                    sp.dma_start(xs(s, ys, ysm), xt_[0:s.rows, s.par, :]).then_inc(y_out[s.par], 16)
                    if loads:
                        alone(sp, y_out[s.par], 16 * (L * (9 - s.par) + s.half + 1))
                        if not last:
                            sp.wait_ge(h_xn, hn(L, s) + 1)
                        load_x(L, s + 2, ys, ysm)

                next_mixed(Step(0))
                o_step(Step(0))
                with sp.Fori(0, (STEPS - 5) // 2) as i:
                    for c in (1, 2):
                        o_step(Step(c, i))
                o_step(E - 3)
                o_step(E - 2, mixed_loads=False)
                o_step(E - 1, False, False)
                o_step(E, False, False)
                alone(sp, y_out[0], 16 * (L + 1) * 9)
                alone(sp, y_out[1], 16 * (L + 1) * 8)
            with sp.Fori(0, DEPTH - 1) as L:
                layer(L, False)
            layer(DEPTH - 1, True)
            sp.wait_ge(kc_out, 2 * DEPTH * 16)
            sp.wait_ge(kvs_out, DEPTH * 256)
            sp.wait_ge(st_out, 64 + DEPTH * 64)
            sp.wait_ge(sts_out, DEPTH * 64)
            sp.wait_ge(kv_out, DEPTH * 32)
            for p in range(2):
                sp.wait_ge(y_out[p], 16 * DEPTH * (9 - p))
                sp.wait_ge(mix_out[p], 16 + 16 * DEPTH * MIX_OUT[p])


ID_LOADS = 1 + DEPTH
CONST_LOADS = 9 + DEPTH * 11
_INS = ["x_prompt", "x_sample", "cache_swa_k", "cache_swa_v", "state_ret", "w_in", "w_out", "norm_g",
        "q_norm_g", "k_norm_g", "sinks"]
_CONSTS = ["rope_ap", "rope_as", "rope_bp", "rope_bs", "mask_a", "mask_s", "decay", "decay_s", "cols", "ident"]
_OUTS = [(1, SEQ, D_MODEL), (DEC_BATCH, DEC_SEQ, D_MODEL),
         (DEPTH, 1, WINDOW, A_KV, A_DIM), (DEPTH, 1, WINDOW, A_KV, A_DIM), (DEPTH, 1, B_HEADS, DK, DV),
         (DEPTH, DEC_BATCH, WINDOW, A_KV, A_DIM), (DEPTH, DEC_BATCH, WINDOW, A_KV, A_DIM),
         (DEPTH, DEC_BATCH, B_HEADS, DK, DV)]


def kernel(**inputs):
    import numpy as _np
    import concourse.bacc as _bacc
    from concourse import mybir as _mybir
    from concourse.bass_utils import run_bass_kernel_spmd as _run

    nc = _bacc.Bacc("TRN2", target_bir_lowering=False, num_devices=1)
    arrays, args = {}, []
    tables = constants()
    for name in _INS + _CONSTS:
        a = _np.ascontiguousarray(inputs[name] if name in _INS else tables[name])
        arrays[f"in_{name}"] = a
        args.append(nc.dram_tensor(f"in_{name}", a.shape, _mybir.dt.from_np(a.dtype), kind="ExternalInput").ap())
    for i, shape in enumerate(_OUTS):
        args.append(nc.dram_tensor(f"out_{i}", shape, _mybir.dt.float32, kind="ExternalOutput").ap())
    args.append(nc.dram_tensor("mixed", (ROWS, MIX_W), _mybir.dt.float32).ap())
    trunk(nc, *args)
    r = _run(nc, [arrays], core_ids=[0])
    return tuple(r.results[0][f"out_{i}"] for i in range(len(_OUTS)))
```
